# Optimizing a Trainium2 kernel written in Bass

```python
import math
import jax, jax.numpy as jnp
from jax import lax
import numpy as np

D_MODEL = 1024
BATCH = 1
SEQ = 256
DEPTH = 1
DEC_BATCH = 8
DEC_SEQ = 8
PAST_LEN = 2048
PAGE_SIZE = 128

HGRN_HEADS = 4
HGRN_DK = 128
HGRN_DV = 128
GLA_HEADS = 4
GLA_DK = 64
GLA_DV = 128
GLA_GATE_RANK = 16
GLA_GATE_NORMALIZER = 16.0
CHUNK = 16
N_EXPERTS = 32
TOP_K = 4
D_FF = D_MODEL
SWIGLU_LIMIT = 7.0
SWIGLU_ALPHA = 1.702
EPS = 1e-6

HK = HGRN_HEADS * HGRN_DK
HV = HGRN_HEADS * HGRN_DV
GK = GLA_HEADS * GLA_DK
GV = GLA_HEADS * GLA_DV
SPLITS = (HK, HK, HV, HV, GK, GK, GV, GLA_GATE_RANK, GV, D_MODEL, D_MODEL)
P_TOTAL = HK + HK + HV + HV + GK + GK + GV + GLA_GATE_RANK + GV + D_MODEL + D_MODEL

kernel_name = "hgrn2_gla_gated_merge_moe_adaln_step"

def _rmsnorm(x, g):
    xf = x.astype(jnp.float32)
    r = lax.rsqrt(jnp.mean(xf * xf, axis=-1, keepdims=True) + EPS)
    return (xf * r).astype(x.dtype) * g

def _gated_linear_recurrence(q, k, v, lg, s0):
    B, T, H, DK = q.shape
    DV = v.shape[-1]
    C = CHUNK
    n = -(-T // C)
    pad = n * C - T
    f32 = jnp.float32
    if pad:
        pw = ((0, 0), (0, pad), (0, 0), (0, 0))
        q, k, v, lg = (jnp.pad(a, pw) for a in (q, k, v, lg))
    q = q.astype(f32).reshape(B, n, C, H, DK)
    k = k.astype(f32).reshape(B, n, C, H, DK)
    v = v.astype(f32).reshape(B, n, C, H, DV)
    b = jnp.cumsum(lg.astype(f32).reshape(B, n, C, H, DK), axis=2)
    causal = jnp.tril(jnp.ones((C, C), dtype=bool))[None, None, :, :, None, None]
    diff = b[:, :, :, None] - b[:, :, None, :]
    decay = jnp.exp(jnp.where(causal, diff, -jnp.inf))
    att = jnp.einsum('bnthd,bnshd,bntshd->bnhts', q, k, decay)
    o_intra = jnp.einsum('bnhts,bnshv->bnthv', att, v)
    b_last = b[:, :, -1]
    k_dec = k * jnp.exp(b_last[:, :, None] - b)
    u = jnp.einsum('bnchd,bnchv->bnhdv', k_dec, v)

    def step(s, inp):
        a, du = inp
        return a[..., None] * s + du, s

    s_final, s_starts = lax.scan(step, s0.astype(f32),
                                 (jnp.moveaxis(jnp.exp(b_last), 1, 0), jnp.moveaxis(u, 1, 0)))
    s_starts = jnp.moveaxis(s_starts, 0, 1)
    o_inter = jnp.einsum('bnchd,bnhdv->bnchv', q * jnp.exp(b), s_starts)
    o = (o_intra + o_inter).reshape(B, n * C, H, DV)[:, :T]
    return o, s_final

def _head_norm_gate(o, gain, gate):
    r = lax.rsqrt(jnp.mean(o * o, axis=-1, keepdims=True) + EPS)
    return o * r * gain.astype(jnp.float32) * jax.nn.silu(gate.astype(jnp.float32))

def _moe(h, r_w, r_b, w_gu, b_gu, w_dn, b_dn):
    logits = (h @ r_w + r_b).astype(jnp.float32)
    top_v, top_i = lax.top_k(logits, TOP_K)
    top_w = jax.nn.softmax(top_v, axis=-1)
    combine = jnp.sum(jax.nn.one_hot(top_i, N_EXPERTS, dtype=jnp.float32) * top_w[..., None], axis=-2)
    combine = combine.astype(h.dtype)
    out = jnp.zeros(h.shape[:-1] + (D_MODEL,), h.dtype)
    for e in range(N_EXPERTS):
        gu = h @ w_gu[e] + b_gu[e]
        gate = jnp.minimum(gu[..., :D_FF], SWIGLU_LIMIT)
        up = jnp.clip(gu[..., D_FF:], -SWIGLU_LIMIT, SWIGLU_LIMIT)
        act = (up + 1.0) * (gate * jax.nn.sigmoid(SWIGLU_ALPHA * gate))
        out = out + combine[..., e:e + 1] * (act @ w_dn[e] + b_dn[e])
    return out

def _trunk_layer(x, c, s_h, s_g, lb, ada_w, ada_b, n1, n2, w_in, hgrn_norm_g,
                 gla_w2, gla_b, gla_norm_g, w_bh, w_bg, w_out, r_w, r_b, w_gu, b_gu, w_dn, b_dn):
    B, T, _ = x.shape
    mod = (jax.nn.silu(c) @ ada_w + ada_b)[:, None, :]
    sh1, sc1, gt1, sh2, sc2, gt2 = jnp.split(mod, 6, axis=-1)

    h = _rmsnorm(x, n1) * (1.0 + sc1) + sh1
    z = h @ w_in
    idx = np.cumsum(np.array(SPLITS))[:-1].tolist()
    hq, hf, hi, hg, gq, gk, gv, gr, gg, ma, mb = jnp.split(z, idx, axis=-1)

    f = lb + (1.0 - lb) * jax.nn.sigmoid(hf.astype(jnp.float32))
    q_h = (jax.nn.silu(hq.astype(jnp.float32)) * HGRN_DK ** -0.5).reshape(B, T, HGRN_HEADS, HGRN_DK)
    k_h = (1.0 - f).reshape(B, T, HGRN_HEADS, HGRN_DK)
    lg_h = jnp.log(f).reshape(B, T, HGRN_HEADS, HGRN_DK)
    v_h = hi.reshape(B, T, HGRN_HEADS, HGRN_DV)
    o_h, s_h_new = _gated_linear_recurrence(q_h, k_h, v_h, lg_h, s_h)
    o_h = _head_norm_gate(o_h, hgrn_norm_g, hg.reshape(B, T, HGRN_HEADS, HGRN_DV))
    o_h = o_h.reshape(B, T, HV).astype(x.dtype)

    lg_g = jax.nn.log_sigmoid((gr @ gla_w2 + gla_b).astype(jnp.float32)) / GLA_GATE_NORMALIZER
    q_g = (gq.astype(jnp.float32) * GLA_DK ** -0.5).reshape(B, T, GLA_HEADS, GLA_DK)
    k_g = gk.reshape(B, T, GLA_HEADS, GLA_DK)
    v_g = gv.reshape(B, T, GLA_HEADS, GLA_DV)
    o_g, s_g_new = _gated_linear_recurrence(q_g, k_g, v_g, lg_g.reshape(B, T, GLA_HEADS, GLA_DK), s_g)
    o_g = _head_norm_gate(o_g, gla_norm_g, gg.reshape(B, T, GLA_HEADS, GLA_DV))
    o_g = o_g.reshape(B, T, GV).astype(x.dtype)

    merged = jax.nn.sigmoid(ma) * (o_h @ w_bh) + jax.nn.sigmoid(mb) * (o_g @ w_bg)
    x = x + gt1 * (merged @ w_out)

    h2 = _rmsnorm(x, n2) * (1.0 + sc2) + sh2
    x = x + gt2 * _moe(h2, r_w, r_b, w_gu, b_gu, w_dn, b_dn)
    return x, s_h_new, s_g_new

def setup_inputs(seed: int = 0) -> dict:
    key = jax.random.key(seed)
    ks = jax.random.split(key, 32)

    def nrm(k, shape, s):
        return jax.random.normal(k, shape, jnp.float32) * s

    D = D_MODEL
    return {
        "x_prompt": nrm(ks[0], (BATCH, SEQ, D), 1.0),
        "x_sample": nrm(ks[1], (DEC_BATCH, DEC_SEQ, D), 1.0),
        "c_prompt": nrm(ks[2], (BATCH, D), 1.0),
        "c_sample": nrm(ks[3], (DEC_BATCH, D), 1.0),
        "state_hgrn": nrm(ks[4], (DEPTH, DEC_BATCH, HGRN_HEADS, HGRN_DK, HGRN_DV), 0.1),
        "state_gla": nrm(ks[5], (DEPTH, DEC_BATCH, GLA_HEADS, GLA_DK, GLA_DV), 0.1),
        "ada_w": nrm(ks[6], (DEPTH, D, 6 * D), 0.5 * D ** -0.5),
        "ada_b": nrm(ks[7], (DEPTH, 6 * D), 0.01),
        "norm1_g": 1.0 + nrm(ks[8], (DEPTH, D), 0.02),
        "norm2_g": 1.0 + nrm(ks[9], (DEPTH, D), 0.02),
        "w_in": nrm(ks[10], (DEPTH, D, P_TOTAL), D ** -0.5),
        "hgrn_lb": 1.0 + nrm(ks[11], (DEPTH + 1, HK), 0.1),
        "hgrn_norm_g": 1.0 + nrm(ks[12], (DEPTH, HGRN_DV), 0.02),
        "gla_gate_w2": nrm(ks[13], (DEPTH, GLA_GATE_RANK, GK), GLA_GATE_RANK ** -0.5),
        "gla_gate_b": nrm(ks[14], (DEPTH, GK), 0.01),
        "gla_norm_g": 1.0 + nrm(ks[15], (DEPTH, GLA_DV), 0.02),
        "w_branch_h": nrm(ks[16], (DEPTH, HV, D), HV ** -0.5),
        "w_branch_g": nrm(ks[17], (DEPTH, GV, D), GV ** -0.5),
        "w_out": nrm(ks[18], (DEPTH, D, D), D ** -0.5),
        "router_w": nrm(ks[19], (DEPTH, D, N_EXPERTS), D ** -0.5),
        "router_b": nrm(ks[20], (DEPTH, N_EXPERTS), 0.01),
        "exp_w_gu": nrm(ks[21], (DEPTH, N_EXPERTS, D, 2 * D_FF), D ** -0.5),
        "exp_b_gu": nrm(ks[22], (DEPTH, N_EXPERTS, 2 * D_FF), 0.01),
        "exp_w_dn": nrm(ks[23], (DEPTH, N_EXPERTS, D_FF, D), D_FF ** -0.5),
        "exp_b_dn": nrm(ks[24], (DEPTH, N_EXPERTS, D), 0.01),
        "final_g": 1.0 + nrm(ks[25], (D,), 0.02),
    }

def reference(x_prompt, x_sample, c_prompt, c_sample, state_hgrn, state_gla, ada_w, ada_b,
              norm1_g, norm2_g, w_in, hgrn_lb, hgrn_norm_g, gla_gate_w2, gla_gate_b, gla_norm_g,
              w_branch_h, w_branch_g, w_out, router_w, router_b, exp_w_gu, exp_b_gu,
              exp_w_dn, exp_b_dn, final_g):
    lbs = jnp.cumsum(jax.nn.softmax(hgrn_lb.astype(jnp.float32), axis=0), axis=0)
    hp, hs = x_prompt, x_sample
    ph, pg, sh, sg = [], [], [], []
    for l in range(DEPTH):
        lw = (ada_w[l], ada_b[l], norm1_g[l], norm2_g[l], w_in[l], hgrn_norm_g[l],
              gla_gate_w2[l], gla_gate_b[l], gla_norm_g[l], w_branch_h[l], w_branch_g[l],
              w_out[l], router_w[l], router_b[l], exp_w_gu[l], exp_b_gu[l], exp_w_dn[l], exp_b_dn[l])
        z_h = jnp.zeros((BATCH, HGRN_HEADS, HGRN_DK, HGRN_DV), jnp.float32)
        z_g = jnp.zeros((BATCH, GLA_HEADS, GLA_DK, GLA_DV), jnp.float32)
        hp, s1, s2 = _trunk_layer(hp, c_prompt, z_h, z_g, lbs[l], *lw)
        hs, s3, s4 = _trunk_layer(hs, c_sample, state_hgrn[l], state_gla[l], lbs[l], *lw)
        ph.append(s1.astype(state_hgrn.dtype))
        pg.append(s2.astype(state_gla.dtype))
        sh.append(s3.astype(state_hgrn.dtype))
        sg.append(s4.astype(state_gla.dtype))
    y_prompt = _rmsnorm(hp, final_g)
    y_sample = _rmsnorm(hs, final_g)
    return (y_prompt, y_sample, jnp.stack(ph), jnp.stack(pg), jnp.stack(sh), jnp.stack(sg))


_drawn_inputs = setup_inputs


def setup_inputs(seed=0):
    import zlib

    import numpy as np

    out = dict(_drawn_inputs(seed))
    spreads = {}
    factors = {'norm2_g': 3.266,
     'hgrn_norm_g': 8.0,
     'gla_gate_b': 8.0,
     'gla_norm_g': 8.0,
     'router_b': 5.639,
     'exp_b_gu': 8.0,
     'exp_b_dn': 61.337,
     'final_g': 7.611}
    for name, (base, spread) in spreads.items():
        noise = np.random.default_rng([zlib.crc32(name.encode()), seed]).standard_normal(out[name].shape)
        drawn = base * np.exp(spread * noise) if base else spread * noise
        out[name] = __import__('jax').numpy.asarray(drawn.astype(out[name].dtype))
    for name, factor in factors.items():
        out[name] = (out[name] * factor).astype(out[name].dtype)
    return out
```

```python
from contextlib import ExitStack

import numpy as np
import concourse.bass as bass
from concourse import mybir

F32 = mybir.dt.float32
BF16 = mybir.dt.bfloat16
I32 = mybir.dt.int32
ACT = mybir.ActivationFunctionType
ALU = mybir.AluOpType
AX = mybir.AxisListType.X
ds = bass.ds

P = 128
D = 1024
DC = D // P
TP, NSEQ, TSQ = 256, 8, 8
T = TP + NSEQ * TSQ
TILES = [(0, 128), (128, 128), (256, 64)]
NROW = 1 + NSEQ
H = 4
RANK = 16
E = 32
TOPK = 4
CAP = 64
CH = 32
NCH = TP // CH
MAXEXTRA = TOPK * T // CAP
NI = E + MAXEXTRA + 1
EPS = 1e-6
LIMIT, ALPHA = 7.0, 1.702
GATE_NORM = 16.0
CLAMP = 40.0
NSLOT, SLOT = 12, 2048
NBANK = 7

CONST_COLS = {}


def _constants():
    cols = []

    def put(name, a):
        b = np.zeros((P, a.shape[1]), np.float32)
        b[:a.shape[0]] = a
        CONST_COLS[name] = (sum(c.shape[1] for c in cols), a.shape[1])
        cols.append(b)

    i = np.arange(P)
    put("ident", np.eye(P))
    put("before", (i[:, None] < i[None, :]).astype(np.float32))
    put("mask_prompt", ((i[:, None] <= i[None, :]) & (i[:, None] // CH == i[None, :] // CH)).astype(np.float32))
    j = np.arange(NSEQ * TSQ)
    put("mask_sample", ((j[:, None] <= j[None, :]) & (j[:, None] // TSQ == j[None, :] // TSQ)).astype(np.float32))
    t = np.arange(T)
    first = np.where(t < TP, t % CH == 0, t % TSQ == 0)
    put("carry", np.tile(np.where(first, 0.0, 1.0), (P, 1)))
    put("seq", (j[:, None] // TSQ == np.arange(NSEQ)[None, :]).astype(np.float32))
    put("slot_no", np.tile(np.arange(P) % CAP, (P, 1)))
    per = P // E
    put("thr", (CAP * (i % per + 1))[:, None])
    put("eid", (i // per)[:, None])
    put("pick96", (np.arange(96)[None, :] % E == (i // per)[:, None]).astype(np.float32))
    put("item_no", np.tile(np.arange(MAXEXTRA + 1), (P, 1)))
    put("items0", np.arange(E)[None, :])
    k = np.arange(96)
    put("own96", (k[:, None] % E == np.arange(E)[None, :]).astype(np.float32))
    put("head_col", np.tile((np.arange(16) == 8).astype(np.float32), (P, 1)))
    return np.concatenate(cols, 1)


CONSTS = _constants()
NCONST = CONSTS.shape[1]
VEC = {"ada_b": (0, 48), "norm1": (48, 8), "norm2": (56, 8), "final": (64, 8), "lb": (72, 8),
       "hgain": (80, 1), "ggain": (81, 1), "gla_b": (82, 2)}
NVEC = 84

GROUPS = [
    (0, 1024, [(f"hq{h}", h * 128, 128) for h in range(4)] + [(f"hf{h}", 512 + h * 128, 128) for h in range(4)]),
    (1024, 1024, [(f"hi{p}", 0, 512) for p in range(3)] + [(f"hg{h}", 512 + h * 128, 128) for h in range(4)]),
    (2048, 1024, [(f"gq{u}", u * 128, 128) for u in range(2)] + [(f"gk{u}", 256 + u * 128, 128) for u in range(2)]
     + [(f"gv{p}", 512, 512) for p in range(3)]),
    (3072, 528, [("gr", 0, 16)] + [(f"gg{h}", 16 + h * 128, 128) for h in range(4)]),
    (3600, 1024, [(f"ma{f}", f * 128, 128) for f in range(8)]),
    (4624, 1024, [(f"mb{f}", f * 128, 128) for f in range(8)]),
]
TURNS = ([(f"ada{i}", "s") for i in range(3)] + [(f"adaT{i}", "v") for i in range(3)] + [("ss1", "v")]
         + [(b[0], "s" if b[0][:2] in ("hi", "gv", "hf") else "v") for g in GROUPS[:4] for b in g[2]]
         + [("low0", "v"), ("low1", "v")]
         + [(b[0], "s") for b in GROUPS[4][2]] + [(b[0], "s") for b in GROUPS[5][2]]
         + [(f"nrm{n}", "v") for n in range(8)]
         + [(f"bh{f}", "v") for f in range(8)] + [(f"bg{f}", "v") for f in range(8)]
         + [(f"out{f}", "v") for f in range(8)] + [("ss2", "v")]
         + [("logits", "v")] + [(f"tok{p}{q}", "s") for p in range(3) for q in range(2)]
         + [("rank", "v"), ("count", "v"), ("place", "v"), ("posT", "v"), ("combT", "v"),
            ("xitems", "v"), ("xpos", "v"), ("xcomb", "v")]
         + [(f"bdn{f}", "v") for f in range(8)])
TURN = {name: n for n, (name, _) in enumerate(TURNS)}
REC_H_AFTER, REC_G_AFTER = TURN["low1"] + 1, TURN["ma7"] + 1


def taken_count(n):
    return sum(1 for _, o in TURNS[:n + 1] if o == TURNS[n][1])


def slot_plan():
    plan, used = [], 0
    groups = ([(f"ada{i}", 8) for i in range(3)] + [(g[2][-1][0], 4) for g in GROUPS]
              + [("bh7", 2), ("bg7", 2), ("out7", 4)])
    for turn, n in groups:
        for s in range(n):
            if s < n - 1:
                used += 1
                plan.append(("used", used))
            else:
                plan.append(("turn", TURN[turn] + 1))
    return plan, used


PLAN, USED0 = slot_plan()
NPRE = len(PLAN)
IT_SLOTS = 12
SLOT0 = NPRE % NSLOT


def build(nc, a):
    ctx = ExitStack()
    with ctx:
        def sb(name, shape, dt=F32):
            return ctx.enter_context(nc.sbuf_tensor(name, shape, dt))

        def sem(name):
            return ctx.enter_context(nc.semaphore(name))

        ring = sb("ring", [P, NSLOT, SLOT])
        xT = sb("xT", [P, DC, T])
        hT = sb("hT", [P, DC, T])
        vtok = sb("vtok", [P, 3, D])
        gates = sb("gates", [P, 2 * H, T])
        big = sb("big", [P, 6 * H * T])
        gla = sb("gla", [P, 3, 2, T])
        consts = sb("consts", [P, NCONST])
        vec = sb("vec", [P, NVEC])
        modT = sb("modT", [P, 48, NROW])
        small = sb("small", [P, 2 * T])
        kdtok = sb("kdtok", [P, 3, P])
        attT = sb("attT", [P, 2, T])
        Sst = sb("Sst", [P, NCH, P])
        S0 = sb("S0", [P, 2, NSEQ, P])
        vblk = sb("vblk", [64, NSEQ, P])
        osq = sb("osq", [P, T])
        ones = sb("ones", [P, P])
        itemtab = sb("itemtab", [1, NI + 1], I32)
        lbt = sb("lbt", [P, 3, H])

        cT = Sst[:, 0:1, :].rearrange("p a b -> p (a b)")[:, 0:DC * NROW].rearrange("p (c r) -> p c r", c=DC)
        csig = Sst[:, 1:2, :].rearrange("p a b -> p (a b)")[:, 0:DC * NROW].rearrange("p (c r) -> p c r", c=DC)
        cpad = Sst[:, 2:4, :].rearrange("p a b -> p (a b)").rearrange("p (c r) -> p c r", c=DC)
        modsb = gates[:, :, :].rearrange("p a b -> p (a b)")[:, 0:1536].rearrange("p (i n) -> p i n", i=3)
        grT = osq[0:RANK, :]
        w2 = S0[0:RANK, 0, 0:2, :].rearrange("p a b -> p (a b)")
        rw = Sst[:, 0:2, :].rearrange("p a b -> p (a b)").rearrange("p (c e) -> p c e", c=DC)
        rb = Sst[0:1, 2, 0:E]
        bdn = S0[0:E, 0, :, :].rearrange("p a b -> p (a b)")

        bigv = big[:, :]

        def cut(at, n):
            return bigv[:, at:at + n]

        HT = H * T

        def units(ap, n):
            return ap.rearrange("p (u t) -> p u t", u=n)

        br = [
            dict(n=4, D=units(cut(0, HT), 4), B=units(cut(HT, HT), 4), q=units(cut(2 * HT, HT), 4),
                 k=units(cut(3 * HT, HT), 4), kd=units(cut(4 * HT, HT), 4), qs=units(cut(5 * HT, HT), 4)),
            dict(n=2, D=gla[:, 0, :, :], B=units(cut(0, 2 * T), 2), q=gla[:, 1, :, :], k=gla[:, 2, :, :],
                 kd=units(cut(2 * T, 2 * T), 2), qs=units(cut(4 * T, 2 * T), 2)),
        ]
        ma = units(cut(4 * HT, 2 * HT), DC)
        mb = units(cut(2 * HT, 2 * HT), DC)
        merged = units(cut(0, 2 * HT), DC)

        def C(name, rows=P):
            at, n = CONST_COLS[name]
            return consts[0:rows, at:at + n]

        def V(name):
            at, n = VEC[name]
            return vec[:, at:at + n]

        off = [0]

        def take(n):
            off[0] += n
            assert off[0] <= 6 * HT
            return cut(off[0] - n, n)

        Sel = take(3 * CAP).rearrange("p (a j) -> p a j", a=3)
        SelW = take(3 * P).rearrange("p (a j) -> p a j", a=3)
        SelWT = take(T)
        gtok = take(512)
        h2g = take(DC * CAP)
        gbuf, ubuf, sbuf_, actb, actT, dng = (take(512) for _ in range(6))
        bgu = take(1024).bitcast(BF16)
        bsel = take(32).bitcast(BF16)
        posI = take(3 * NI).rearrange("p (a i) -> p a i", a=3)
        wI = take(3 * NI).rearrange("p (a i) -> p a i", a=3)
        OHI = take(NI)
        yacc = gates
        h2tok = vtok
        rt = gla[:, :, :, :].rearrange("p a b c -> p (a b c)")
        roff = [0]

        def rtake(n, k=3):
            roff[0] += n * k
            assert roff[0] <= 6 * T
            return rt[:, roff[0] - n * k:roff[0]].rearrange("p (a e) -> p a e", a=k)

        Lg, sel, comb, eqm, cum, m1, posm = (rtake(E) for _ in range(7))
        top8 = rtake(8)
        tot = rtake(1)
        ngt = rtake(1)
        selx = rtake(P)
        flag, slotq = rtake(1, 1), rtake(1, 1)
        Oq = rtake(MAXEXTRA + 1, 1)
        posT = small[0:E, 0:T]
        combT = small[0:E, T:2 * T]
        thrrep = rtake(P, 1)
        frow = rtake(MAXEXTRA + 1, 1)
        bguf = hT[0:96, :, :].rearrange("p a b -> p (a b)")[:, 0:2048]

        banks = [ctx.enter_context(nc.psum_tensor(f"bank{n}", [P, 512], F32)) for n in range(8)]

        slot_landed = [sem(f"slot_landed{n}") for n in range(NSLOT)]
        slot_used = sem("slot_used")
        turn_filled = sem("turn_filled")
        taken = {"v": sem("turn_taken_by_vector"), "s": sem("turn_taken_by_scalar")}
        x_landed, c_landed, consts_landed, w2_landed = sem("x_landed"), sem("c_landed"), sem("consts_landed"), sem("w2_landed")
        router_landed, bgu_landed, bdn_landed = sem("router_landed"), sem("bgu_landed"), sem("bdn_landed")
        state_landed = [sem("state_landed0"), sem("state_landed1")]
        ones_set, pads_set = sem("ones_set"), sem("pads_set")
        csig_ready, cond_ready = sem("csig_ready"), sem("cond_ready")
        xsq_ready, root_wanted, root_ready = sem("xsq_ready"), sem("root_wanted"), sem("root_ready")
        h_ready = sem("h_ready")
        lbexp_wanted, lbexp_ready = sem("lbexp_wanted"), sem("lbexp_ready")
        sig_ready = sem("sig_ready")
        exp_wanted, exp_ready = sem("exp_wanted"), sem("exp_ready")
        ops_ready = sem("ops_ready")
        low_wanted, low_ready = sem("low_wanted"), sem("low_ready")
        kd_flipped, kd_copied = sem("kd_flipped"), sem("kd_copied")
        att_ready, att_masked = sem("att_ready"), sem("att_masked")
        u_ready, chain_done = sem("u_ready"), sem("chain_done")
        o_ready, o_squared, o_summed, o_gated = sem("o_ready"), sem("o_squared"), sem("o_summed"), sem("o_gated")
        vblk_ready, su_ready, su_added = sem("vblk_ready"), sem("su_ready"), sem("su_added")
        prompt_state_out, sample_state_out, y_out = sem("prompt_state_out"), sem("sample_state_out"), sem("y_out")
        norms_done, merged_done, h2_ready = sem("norms_done"), sem("merged_done"), sem("h2_ready")
        sel_routed, thr_ready, oq_ready, xoh_ready = (sem("sel_routed"), sem("thr_ready"), sem("oq_ready"),
                                                                   sem("xoh_ready"))
        rexp_wanted, rexp_ready = sem("rexp_wanted"), sem("rexp_ready")
        comb_ready = sem("comb_ready")
        sel_ready, gathered, gtok_copied = sem("sel_ready"), sem("gathered"), sem("gtok_copied")
        gtok_flipped, h2g_copied = sem("gtok_flipped"), sem("h2g_copied")
        bsel_ready, gate_ready, up_ready = sem("bsel_ready"), sem("gate_ready"), sem("up_ready")
        gate_clamped, swish_ready, act_ready = sem("gate_clamped"), sem("swish_ready"), sem("act_ready")
        selw_ready, selw_flipped, selw_copied = sem("selw_ready"), sem("selw_flipped"), sem("selw_copied")
        act_flipped, act_copied, dn_ready, dn_copied = sem("act_flipped"), sem("act_copied"), sem("dn_ready"), sem("dn_copied")
        scattered, summed = sem("scattered"), sem("summed")
        x3sq_ready, ss3_ready, root3_wanted, root3_ready, y_ready = (sem("x3sq_ready"), sem("ss3_ready"), sem("root3_wanted"),
                                                                    sem("root3_ready"), sem("y_ready"))
        vector_step, scalar_step = sem("vector_step"), sem("scalar_step")

        block = ctx.enter_context(nc.Block())

        class Steps:

            def __init__(self, eng, sem_):
                self.eng, self.sem, self.n, self.base = eng, sem_, 0, 0

            def then_wait(self, ins):
                ins.then_inc(self.sem, 1)
                self.n += 1
                self.eng.wait_ge(self.sem, self.base + self.n)

        def wait_taken(eng, n):
            owner = TURNS[n][1]
            eng.wait_ge(taken[owner], taken_count(n))

        def bank_of(name):
            return banks[TURN[name] % NBANK]

        def wait_filled(eng, name):
            eng.wait_ge(turn_filled, TURN[name] + 1)

        def landed(eng, n):
            eng.wait_ge(slot_landed[n % NSLOT], 16 * (n // NSLOT + 1))

        def item_slot(s):
            return (SLOT0 + s) % NSLOT

        def item_landed_count(s):
            return 16 * ((NPRE + s) // NSLOT + 1)

        def pair(n):
            return ring[:, n % NSLOT, :].rearrange("p (k c) -> p k c", k=2)

        HEADS = [(0, u, 0, u, 0, 128) for u in range(4)] + [(1, u, hh, 4 + 2 * u + hh, 64 * hh, 64)
                                                             for u in range(2) for hh in range(2)]
        UNITS = [(b, u) for b in range(2) for u in range(br[b]["n"])]
        FIRSTHEAD = [0, 1, 2, 3, 4, 6]
        SCATTER = [3, 5, 0, 4, 6, 7, 6, 7]

        @block.sync
        def _(sp):
            n = 0

            def wait_slot(m):
                if m >= NSLOT:
                    kind, val = PLAN[m - NSLOT]
                    sp.wait_ge(slot_used if kind == "used" else turn_filled, val)

            def stream(src, dst):
                nonlocal n
                wait_slot(n)
                sp.dma_start(dst, src).then_inc(slot_landed[n % NSLOT], 16)
                n += 1

            for i in range(3):
                for k in range(DC):
                    stream(a["ada_w"][0, k * P:(k + 1) * P, i * SLOT:(i + 1) * SLOT], ring[:, n % NSLOT, :])
            for c0, w, _ in GROUPS:
                for s in range(4):
                    stream(a["w_in"][0, 2 * s * P:(2 * s + 2) * P, c0:c0 + w].rearrange("(k p) c -> p k c", p=P),
                           pair(n)[:, :, 0:w])
            for name, cnt in (("w_branch_h", 2), ("w_branch_g", 2), ("w_out", 4)):
                for s in range(cnt):
                    stream(a[name][0, 2 * s * P:(2 * s + 2) * P, :].rearrange("(k p) c -> p k c", p=P), pair(n))
            assert n == NPRE

            def item(i, e):
                for s in range(IT_SLOTS):
                    if i is None:
                        wait_slot(NPRE + s)
                    elif s == 7:
                        sp.wait_ge(up_ready, i)
                    elif s == 11:
                        sp.wait_ge(dn_ready, i)
                    else:
                        sp.wait_ge(slot_used, (i - 1) * 10 + (USED0 + (s if s < 7 else s - 1) + 1))
                    if s < DC:
                        src = a["exp_w_gu"][0, ds(e, 1), s * P:(s + 1) * P, :].rearrange("a p c -> p (a c)")
                        dst = ring[:, item_slot(s), :]
                    else:
                        k = 2 * (s - DC)
                        src = a["exp_w_dn"][0, ds(e, 1), k * P:(k + 2) * P, :].rearrange("a (k p) c -> p (a k) c", p=P)
                        dst = pair(item_slot(s))
                    sp.dma_start(dst, src).then_inc(slot_landed[item_slot(s)], 16)

            item(None, 0)
            wait_taken(sp, TURN["xitems"])
            count = sp.value_load(itemtab[0:1, NI:NI + 1], min_val=0, max_val=MAXEXTRA) + E
            with sp.Fori(1, count) as i:
                e = sp.value_load(itemtab[0:1, ds(i, 1)], min_val=0, max_val=E - 1)
                item(i, e)
            sp.wait_ge(y_ready, 1)
            sp.dma_start(a["yT"], xT[:, :, :]).then_inc(y_out, 16)
            sp.wait_ge(y_out, 16)

        @block.gpsimd
        def _(pool):
            def load_state(ui):
                b, u = UNITS[ui]
                buf = S0[:, ui % 2, :, :]
                if b == 0:
                    src = a["state_hgrn"][0, :, u, :, :].rearrange("b k v -> k b v")
                    pool.dma_start(buf, src).then_inc(state_landed[ui % 2], 16)
                else:
                    for hh in range(2):
                        src = a["state_gla"][0, :, 2 * u + hh, :, :].rearrange("b k v -> k b v")
                        pool.dma_start(buf[64 * hh:64 * hh + 64, :, :], src).then_inc(state_landed[ui % 2], 16)

            pool.dma_start(w2, a["gla_w2"]).then_inc(w2_landed, 16)
            load_state(1)
            wait_filled(pool, "low1")
            load_state(0)
            outs_s = [0, 0]
            for ui, (b, u) in enumerate(UNITS):
                for (hb, hu, hh, n, p0, dk) in HEADS:
                    if (hb, hu) != (b, u):
                        continue
                    wait_taken(pool, TURN["hi2" if b == 0 else "gv2"])
                    pool.wait_ge(consts_landed, 32)
                    if n:
                        pool.wait_ge(su_ready, n)
                    v = vtok[0:64, 2, n * P:(n + 1) * P].unsqueeze(1).broadcast_to([64, NSEQ, P])
                    m = C("seq", 64).unsqueeze(2).broadcast_to([64, NSEQ, P])
                    nc.gpsimd.tensor_tensor(vblk[:, :, :], v, m, ALU.mult).then_inc(vblk_ready, 1)
                pool.wait_ge(chain_done, ui + 1)
                if b == 0:
                    pool.dma_start(a["hgrn_prompt"][0, 0, u, :, :], Sst[:, NCH - 1, :]).then_inc(prompt_state_out, 16)
                else:
                    for hh in range(2):
                        pool.dma_start(a["gla_prompt"][0, 0, 2 * u + hh, :, :],
                                       Sst[64 * hh:64 * hh + 64, NCH - 1, :]).then_inc(prompt_state_out, 16)
                last = FIRSTHEAD[ui + 1] if ui + 1 < len(UNITS) else len(HEADS)
                pool.wait_ge(su_added, last)
                buf = S0[:, ui % 2, :, :]
                if b == 0:
                    pool.dma_start(a["hgrn_sample"][0, :, u, :, :].rearrange("b k v -> k b v"), buf).then_inc(sample_state_out, 16)
                    outs_s[0] += 16
                else:
                    for hh in range(2):
                        pool.dma_start(a["gla_sample"][0, :, 2 * u + hh, :, :].rearrange("b k v -> k b v"),
                                       buf[64 * hh:64 * hh + 64, :, :]).then_inc(sample_state_out, 16)
                        outs_s[0] += 16
                if ui + 2 < len(UNITS):
                    pool.wait_ge(sample_state_out, outs_s[0])
                    load_state(ui + 2)
            pool.wait_ge(sample_state_out, outs_s[0])
            pool.wait_ge(prompt_state_out, 16 * 4 + 32 * 2)
            pool.dma_start(rw, a["router_w"]).then_inc(router_landed, 16)
            pool.dma_start(rb, a["router_b"]).then_inc(router_landed, 16)
            pool.dma_start(bdn, a["exp_b_dn"][0, :, :]).then_inc(bdn_landed, 16)
            wait_filled(pool, "tok21")
            for g in range(3):
                pool.dma_start(bguf[32 * g:32 * g + 32, :], a["exp_b_gu"][0, :, :]).then_inc(bgu_landed, 16)

        @block.tensor
        def _(pe):
            mm = nc.tensor.matmul
            ident = C("ident")
            slot = [0]

            def open_turn(name):
                n = TURN[name]
                m = n - NBANK
                if m >= 0:
                    wait_taken(pe, m)
                return banks[n % NBANK]

            pe.wait_ge(cond_ready, 1)
            for i in range(3):
                b = open_turn(f"ada{i}")
                for k in range(DC):
                    landed(pe, slot[0])
                    for g in range(4):
                        last = mm(b[32 * g:32 * g + 32, :], cpad[:, k, :], ring[:, slot[0] % NSLOT, g * 512:(g + 1) * 512],
                                  start=(k == 0), stop=(k == DC - 1))
                    last.then_inc(slot_used if k < DC - 1 else turn_filled, 1)
                    slot[0] += 1
            pe.wait_ge(consts_landed, 32)
            for i in range(3):
                b = open_turn(f"adaT{i}")
                wait_taken(pe, TURN[f"ada{i}"])
                for j in range(4):
                    last = nc.tensor.transpose(b[:, j * P:(j + 1) * P], modsb[:, i, j * P:(j + 1) * P], ident)
                last.then_inc(turn_filled, 1)

            def sum_squares(name, src):
                b = open_turn(name)
                for k in range(DC):
                    last = mm(b[:, 0:T], ones[:, :], src[:, k, :], start=(k == 0), stop=(k == DC - 1))
                last.then_inc(turn_filled, 1)

            pe.wait_ge(ones_set, 1)
            pe.wait_ge(xsq_ready, 1)
            sum_squares("ss1", hT)

            def group(gi):
                s0 = slot[0]
                blocks = GROUPS[gi][2]
                for bi, (name, c, w) in enumerate(blocks):
                    b = open_turn(name)
                    for k in range(DC):
                        if bi == 0 and k % 2 == 0:
                            landed(pe, s0 + k // 2)
                        wts = pair(s0 + k // 2)[:, k % 2, c:c + w]
                        if name[:2] in ("hi", "gv"):
                            t0, tn = TILES[int(name[2])]
                            ins = mm(b[0:tn, :], hT[:, k, t0:t0 + tn], wts, start=(k == 0), stop=(k == DC - 1))
                        else:
                            ins = mm(b[0:w, 0:T], wts, hT[:, k, :], start=(k == 0), stop=(k == DC - 1))
                        if k == DC - 1:
                            ins.then_inc(turn_filled, 1)
                        elif bi == len(blocks) - 1 and k % 2:
                            ins.then_inc(slot_used, 1)
                slot[0] += 4

            pe.wait_ge(h_ready, 1)
            for gi in range(4):
                group(gi)
            pe.wait_ge(w2_landed, 16)
            wait_taken(pe, TURN["gr"])
            for u in range(2):
                b = open_turn(f"low{u}")
                mm(b[:, 0:T], w2[:, u * P:(u + 1) * P], grT, start=True, stop=True).then_inc(turn_filled, 1)

            def wait_all_turns(upto):
                for o in "vs":
                    pe.wait_ge(taken[o], sum(1 for _, x in TURNS[:upto] if x == o))

            bATT, bKD, bO, bU = banks[0], banks[1], banks[2], banks[3:7]

            def recurrence(bi):
                pe.wait_ge(ops_ready, bi + 1)
                pe.wait_ge(pads_set, 1)
                for ui, (b, u) in enumerate(UNITS):
                    if b != bi:
                        continue
                    o = br[b]
                    heads = [h for h in HEADS if h[0] == b and h[1] == u]
                    if ui:
                        pe.wait_ge(kd_copied, ui)
                    for p, (t0, tn) in enumerate(TILES):
                        last = nc.tensor.transpose(bKD[0:tn, p * P:(p + 1) * P], o["kd"][:, u, t0:t0 + tn], ident)
                    last.then_inc(kd_flipped, 1)
                    for (_, _, hh, n, p0, dk) in heads:
                        if n:
                            pe.wait_ge(att_masked, n)
                        for t0, tn in TILES:
                            last = mm(bATT[0:tn, t0:t0 + tn], o["k"][p0:p0 + dk, u, t0:t0 + tn],
                                      o["qs"][p0:p0 + dk, u, t0:t0 + tn], start=True, stop=True)
                        last.then_inc(att_ready, 1)
                    pe.wait_ge(kd_copied, ui + 1)
                    if ui:
                        pe.wait_ge(su_added, heads[0][3])
                    for c in range(NCH):
                        r0, p = CH * (c % 4), c // 4
                        for (_, _, hh, n, p0, dk) in heads:
                            last = mm(bU[c % 4][p0:p0 + dk, p * P:(p + 1) * P], kdtok[r0:r0 + CH, p, p0:p0 + dk],
                                      vtok[r0:r0 + CH, p, n * P:(n + 1) * P], start=True, stop=True,
                                      tile_position=(r0, p0))
                    last.then_inc(u_ready, 1)
                    pe.wait_ge(chain_done, ui + 1)
                    pe.wait_ge(state_landed[ui % 2], [16, 16, 32, 32, 64, 64][ui])
                    for (_, _, hh, n, p0, dk) in heads:
                        pe.wait_ge(att_masked, n + 1)
                        if n:
                            pe.wait_ge(o_gated, n)
                        for p, (t0, tn) in enumerate(TILES):
                            mm(bO[:, t0:t0 + tn], vtok[:, p, n * P:(n + 1) * P], attT[:, hh, t0:t0 + tn],
                               start=(p == 0), stop=False, skip_group_check=True)
                        for c in range(1, NCH):
                            mm(bO[:, c * CH:(c + 1) * CH], Sst[p0:p0 + dk, c - 1, :], o["q"][p0:p0 + dk, u, c * CH:(c + 1) * CH],
                               start=False, stop=False, skip_group_check=True)
                        for s in range(NSEQ):
                            t0 = TP + s * TSQ
                            last = mm(bO[:, t0:t0 + TSQ], S0[p0:p0 + dk, ui % 2, s, :], o["q"][p0:p0 + dk, u, t0:t0 + TSQ],
                                      start=False, stop=(s == NSEQ - 1), skip_group_check=True)
                        last.then_inc(o_ready, 1)
                        pe.wait_ge(vblk_ready, n + 1)
                        if n and hh:
                            pe.wait_ge(su_added, n)
                        for x in range(2):
                            last = mm(bU[x][p0:p0 + dk, :], kdtok[0:64, 2, p0:p0 + dk],
                                      vblk[:, 4 * x:4 * x + 4, :].rearrange("p a b -> p (a b)"), start=True, stop=True,
                                      tile_position=(0, p0))
                        last.then_inc(su_ready, 1)
                        pe.wait_ge(o_squared, n + 1)
                        at = CONST_COLS["head_col"][0] + 8 - n
                        mm(banks[7][0:8, 0:T], consts[:, at:at + 8], osq[:, :], start=(n == 0), stop=(n == 7))\
                            .then_inc(o_summed, 1)

            wait_all_turns(REC_H_AFTER)
            recurrence(0)
            pe.wait_ge(o_gated, 4)
            pe.wait_ge(su_added, 4)
            group(4)
            wait_all_turns(REC_G_AFTER)
            recurrence(1)
            pe.wait_ge(o_gated, 8)
            pe.wait_ge(su_added, 8)
            group(5)
            pe.wait_ge(norms_done, 1)
            for n in range(8):
                b = open_turn(f"nrm{n}")
                mm(b[:, 0:T], ident[0:8, n:n + 1].broadcast_to([8, P]), small[0:8, 0:T], start=True, stop=True)\
                    .then_inc(turn_filled, 1)
            wait_taken(pe, TURN["nrm7"])
            for bi, pre in enumerate(("bh", "bg")):
                s0 = slot[0]
                landed(pe, s0)
                landed(pe, s0 + 1)
                for f in range(DC):
                    b = open_turn(f"{pre}{f}")
                    for k in range(H):
                        ins = mm(b[:, 0:T], pair(s0 + k // 2)[:, k % 2, f * P:(f + 1) * P], gates[:, 4 * bi + k, :],
                                 start=(k == 0), stop=(k == H - 1))
                        if k == H - 1:
                            ins.then_inc(turn_filled, 1)
                        elif f == DC - 1 and k == 1:
                            ins.then_inc(slot_used, 1)
                slot[0] += 2
            pe.wait_ge(merged_done, 1)
            s0 = slot[0]
            for f in range(DC):
                b = open_turn(f"out{f}")
                for k in range(DC):
                    if f == 0 and k % 2 == 0:
                        landed(pe, s0 + k // 2)
                    ins = mm(b[:, 0:T], pair(s0 + k // 2)[:, k % 2, f * P:(f + 1) * P], merged[:, k, :],
                             start=(k == 0), stop=(k == DC - 1))
                    if k == DC - 1:
                        ins.then_inc(turn_filled, 1)
                    elif f == DC - 1 and k % 2:
                        ins.then_inc(slot_used, 1)
            pe.wait_ge(xsq_ready, 2)
            sum_squares("ss2", hT)

            pe.wait_ge(h2_ready, 1)
            pe.wait_ge(router_landed, 32)
            b = open_turn("logits")
            for p, (t0, tn) in enumerate(TILES):
                for k in range(DC):
                    mm(b[0:tn, p * E:(p + 1) * E], hT[:, k, t0:t0 + tn], rw[:, k, :], start=(k == 0), stop=False)
                last = mm(b[0:tn, p * E:(p + 1) * E], ones[0:1, 0:tn], rb, start=False, stop=True)
            last.then_inc(turn_filled, 1)
            for p, (t0, tn) in enumerate(TILES):
                for q in range(2):
                    b = open_turn(f"tok{p}{q}")
                    for j in range(4):
                        last = nc.tensor.transpose(b[0:tn, j * P:(j + 1) * P], hT[:, 4 * q + j, t0:t0 + tn], ident)
                    last.then_inc(turn_filled, 1)
            pe.wait_ge(sel_routed, 1)
            b = open_turn("rank")
            for p in range(3):
                for s in range(p + 1):
                    last = mm(b[:, p * E:(p + 1) * E], C("before") if s == p else ones[:, :], sel[:, s, :],
                              start=(s == 0), stop=(s == p))
            last.then_inc(turn_filled, 1)
            b = open_turn("count")
            for s in range(3):
                last = mm(b[:, 0:1], selx[:, s, :], ones[:, 0:1], start=(s == 0), stop=(s == 2))
            last.then_inc(turn_filled, 1)
            wait_taken(pe, TURN["count"])
            b = open_turn("place")
            mm(b[:, 0:1], C("before"), flag[:, 0, :], start=True, stop=True)
            mm(b[0:1, 1:2], flag[:, 0, :], ones[:, 0:1], start=True, stop=True).then_inc(turn_filled, 1)
            pe.wait_ge(comb_ready, 1)
            for name, src in (("posT", posm), ("combT", comb)):
                b = open_turn(name)
                for p, (t0, tn) in enumerate(TILES):
                    last = nc.tensor.transpose(b[0:E, t0:t0 + tn], src[0:tn, p, :], ident[0:tn, 0:tn])
                last.then_inc(turn_filled, 1)
            pe.wait_ge(oq_ready, 1)
            pe.wait_ge(thr_ready, 1)
            b = open_turn("xitems")
            X = MAXEXTRA + 1
            mm(b[0:96, 0:X], C("pick96"), Oq[:, 0, :], start=True, stop=True)
            mm(b[0:1, 32:32 + X], C("eid"), Oq[:, 0, :], start=True, stop=True)
            mm(b[:, 64:64 + X], thrrep[:, 0, :], Oq[:, 0, :], start=True, stop=True).then_inc(turn_filled, 1)
            pe.wait_ge(xoh_ready, 1)
            for name, src in (("xpos", posT), ("xcomb", combT)):
                b = open_turn(name)
                for p, (t0, tn) in enumerate(TILES):
                    last = mm(b[0:tn, p * X:(p + 1) * X], src[:, t0:t0 + tn], OHI[0:E, E:NI], start=True, stop=True)
                last.then_inc(turn_filled, 1)
            pe.wait_ge(bdn_landed, 16)
            for f in range(DC):
                b = open_turn(f"bdn{f}")
                mm(b[:, 0:T], bdn[:, f * P:(f + 1) * P], combT, start=True, stop=True).then_inc(turn_filled, 1)
            wait_all_turns(len(TURNS))

            def half(k):
                at = (k % 4) * P + (k // 4) * CAP
                return slice(at, at + CAP)

            def gather(j):
                pe.wait_ge(sel_ready, j + 1)
                for p in range(3):
                    for h in range(2):
                        last = mm(banks[0][64 * h:64 * h + 64, :], Sel[:, p, :], h2tok[:, p, h * 512:(h + 1) * 512],
                                  start=(p == 0), stop=(p == 2))
                last.then_inc(gathered, 1)

            def flip_gathered(j):
                pe.wait_ge(gtok_copied, j + 1)
                for x in range(4):
                    last = nc.tensor.transpose(banks[0][:, x * P:(x + 1) * P], gtok[:, x * P:(x + 1) * P], ident)
                last.then_inc(gtok_flipped, 1)

            def scatter(i):
                pe.wait_ge(dn_copied, i + 1)
                pe.wait_ge(selw_copied, i + 1)
                for n in range(8):
                    q, h = n // 2, n % 2
                    if n == 0:
                        pe.wait_ge(summed, i * 8 + 1)
                    if n >= 6:
                        pe.wait_ge(summed, i * 8 + (n - 2 + 2))
                    mm(banks[SCATTER[n]][:, 0:T], dng[64 * h:64 * h + 64, q * P:(q + 1) * P], SelWT[64 * h:64 * h + 64, :],
                       start=True, stop=True).then_inc(scattered, 1)

            def item(i, first):
                pe.wait_ge(h2g_copied, i + 1)
                pe.wait_ge(bsel_ready, i + 1)
                if not first:
                    pe.wait_ge(gate_clamped, i)
                    pe.wait_ge(act_ready, i)
                for m in range(2):
                    for h in range(2):
                        mm(banks[1 + m][64 * h:64 * h + 64, :], bsel[0:96, :], bgu[0:96, m * D + h * 512:m * D + (h + 1) * 512],
                           start=True, stop=False)
                for k in range(DC):
                    pe.wait_ge(slot_landed[item_slot(k)], i * 16 + item_landed_count(k))
                    for m in range(2):
                        for h in range(2):
                            c = m * D + h * 512
                            ins = mm(banks[1 + m][64 * h:64 * h + 64, :], h2g[:, half(k)],
                                     ring[:, item_slot(k), c:c + 512], start=False, stop=(k == DC - 1))
                        if k == DC - 1:
                            ins.then_inc(up_ready if m else gate_ready, 1)
                        elif m:
                            ins.then_inc(slot_used, 1)
                if not first:
                    scatter(i - 1)
                pe.wait_ge(selw_ready, i + 1)
                if not first:
                    pe.wait_ge(summed, i * 8 - 8 + 3)
                for p, (t0, tn) in enumerate(TILES):
                    last = nc.tensor.transpose(banks[5][:, t0:t0 + tn], SelW[0:tn, p, :], ident[0:tn, 0:tn])
                last.then_inc(selw_flipped, 1)
                pe.wait_ge(act_ready, i + 1)
                for j in range(4):
                    last = nc.tensor.transpose(banks[3][:, j * P:(j + 1) * P], actb[:, j * P:(j + 1) * P], ident)
                last.then_inc(act_flipped, 1)
                if not first:
                    pe.wait_ge(summed, i * 8 - 8 + 5)
                gather(i + 1)
                pe.wait_ge(act_copied, i + 1)
                for k in range(DC):
                    if k % 2 == 0:
                        s = DC + k // 2
                        pe.wait_ge(slot_landed[item_slot(s)], i * 16 + item_landed_count(s))
                    for h in range(2):
                        ins = mm(banks[4][64 * h:64 * h + 64, :], actT[:, half(k)],
                                 pair(item_slot(DC + k // 2))[:, k % 2, h * 512:(h + 1) * 512],
                                 start=(k == 0), stop=(k == DC - 1))
                    if k == 5:
                        ins.then_inc(slot_used, 1)
                        flip_gathered(i + 1)
                        continue
                    if k == DC - 1:
                        ins.then_inc(dn_ready, 1)
                    elif k % 2:
                        ins.then_inc(slot_used, 1)

            wait_taken(pe, TURN["xitems"])
            count = pe.value_load(itemtab[0:1, NI:NI + 1], min_val=0, max_val=MAXEXTRA) + E
            gather(0)
            flip_gathered(0)
            item(0, True)
            with pe.Fori(1, count) as i:
                item(i, False)
            scatter(count - 1)
            pe.wait_ge(x3sq_ready, 1)
            for k in range(DC):
                last = mm(banks[0][:, 0:T], ones[:, :], hT[:, k, :], start=(k == 0), stop=(k == DC - 1))
            last.then_inc(ss3_ready, 1)

        @block.scalar
        def _(act):
            S = Steps(act, scalar_step)
            A = nc.scalar.activation
            act.dma_start(cT, a["cT"]).then_inc(c_landed, 16)
            act.dma_start(xT[:, :, :], a["xT"]).then_inc(x_landed, 16)
            act.dma_start(consts[:, :], a["consts"]).then_inc(consts_landed, 16)
            act.dma_start(vec[:, :], a["vec"]).then_inc(consts_landed, 16)
            act.wait_ge(c_landed, 16)
            A(csig, cT, ACT.Sigmoid).then_inc(csig_ready, 1)
            act.wait_ge(x_landed, 16)
            A(hT[:, :, :], xT[:, :, :], ACT.Square).then_inc(xsq_ready, 1)
            for i in range(3):
                wait_filled(act, f"ada{i}")
                A(modsb[:, i, :], bank_of(f"ada{i}")[:, :], ACT.Copy).then_inc(taken["s"], 1)
            act.wait_ge(lbexp_wanted, 1)
            A(lbt[:, 0:2, :], lbt[:, 0:2, :], ACT.Exp).then_inc(lbexp_ready, 1)
            wait_taken(act, TURN["ss1"])
            A(small[:, 0:T], small[:, 0:T], ACT.Sqrt).then_inc(root_ready, 1)

            scratch, sig_names = [0], []

            def sig_scratch(name):
                m = scratch[0]
                wait_filled(act, name)
                if m >= 2:
                    wait_taken(act, TURN[sig_names[m - 2]])
                else:
                    act.wait_ge(h_ready, 1)
                sig_names.append(name)
                A(small[:, (m % 2) * T:(m % 2 + 1) * T], bank_of(name)[:, 0:T], ACT.Sigmoid).then_inc(sig_ready, 1)
                scratch[0] += 1

            for u in range(4):
                sig_scratch(f"hq{u}")
            for u in range(4):
                wait_filled(act, f"hf{u}")
                A(br[0]["k"][:, u, :], bank_of(f"hf{u}")[:, 0:T], ACT.Sigmoid).then_inc(taken["s"], 1)

            def branch_exps(bi):
                o = br[bi]
                w0 = 3 * bi
                if bi == 0:
                    act.wait_ge(exp_wanted, 1)
                    A(o["D"], o["D"], ACT.Ln).then_inc(exp_ready, 1)
                for j, (dst, sign) in enumerate((("D", 1.0), ("qs", 1.0), ("D", -1.0), ("D", 1.0))):
                    src = "D" if j < 3 else "B"
                    act.wait_ge(exp_wanted, w0 + (2, 3, 3, 4)[j])
                    if j == 2:
                        act.wait_ge(exp_ready, 6 + 1 if bi else 3)
                    A(o[dst], o[src], ACT.Exp, scale=sign).then_inc(exp_ready, 1)

            branch_exps(0)
            for p in range(3):
                wait_filled(act, f"hi{p}")
                tn = TILES[p][1]
                A(vtok[0:tn, p, 0:512], bank_of(f"hi{p}")[0:tn, :], ACT.Copy).then_inc(taken["s"], 1)
            for u in range(4):
                sig_scratch(f"hg{u}")
            for p in range(3):
                wait_filled(act, f"gv{p}")
                tn = TILES[p][1]
                A(vtok[0:tn, p, 512:1024], bank_of(f"gv{p}")[0:tn, :], ACT.Copy).then_inc(taken["s"], 1)
            for u in range(4):
                sig_scratch(f"gg{u}")
            act.wait_ge(low_wanted, 1)
            S.then_wait(A(br[1]["D"], br[1]["D"], ACT.Exp))
            A(br[1]["D"], br[1]["D"], ACT.Ln, bias=1.0).then_inc(low_ready, 1)

            def recurrence(bi):
                for ui, (b, u) in enumerate(UNITS):
                    if b != bi:
                        continue
                    heads = [h for h in HEADS if h[0] == b and h[1] == u]
                    act.wait_ge(kd_flipped, ui + 1)
                    if ui:
                        act.wait_ge(su_ready, heads[0][3])
                    A(kdtok[:, 0:2, :].rearrange("p a b -> p (a b)"), banks[1][:, 0:2 * P], ACT.Copy)
                    A(kdtok[0:64, 2, :], banks[1][0:64, 2 * P:3 * P], ACT.Copy).then_inc(kd_copied, 1)
                    for h in heads:
                        n = h[3]
                        act.wait_ge(o_ready, n + 1)
                        if n:
                            act.wait_ge(o_summed, n)
                        A(osq[:, :], banks[2][:, 0:T], ACT.Square).then_inc(o_squared, 1)

            recurrence(0)
            for f in range(DC):
                wait_filled(act, f"ma{f}")
                A(ma[:, f, :], bank_of(f"ma{f}")[:, 0:T], ACT.Sigmoid).then_inc(taken["s"], 1)
            branch_exps(1)
            recurrence(1)
            for f in range(DC):
                wait_filled(act, f"mb{f}")
                A(mb[:, f, :], bank_of(f"mb{f}")[:, 0:T], ACT.Sigmoid).then_inc(taken["s"], 1)
            act.wait_ge(root_wanted, 1)
            A(small[0:8, 0:T], small[0:8, 0:T], ACT.Sqrt).then_inc(root_ready, 1)
            act.wait_ge(merged_done, 2)
            A(hT[:, :, :], xT[:, :, :], ACT.Square).then_inc(xsq_ready, 1)
            wait_taken(act, TURN["ss2"])
            A(small[:, 0:T], small[:, 0:T], ACT.Sqrt).then_inc(root_ready, 1)
            act.wait_ge(rexp_wanted, 1)
            A(comb, comb, ACT.Exp).then_inc(rexp_ready, 1)
            for p, (t0, tn) in enumerate(TILES):
                for q in range(2):
                    wait_filled(act, f"tok{p}{q}")
                    A(h2tok[0:tn, p, q * 512:(q + 1) * 512], bank_of(f"tok{p}{q}")[0:tn, :], ACT.Copy).then_inc(taken["s"], 1)

            def copy_gathered(j):
                act.wait_ge(gathered, j + 1)
                A(gtok, banks[0][:, :], ACT.Copy).then_inc(gtok_copied, 1)

            def copy_flipped(j):
                act.wait_ge(gtok_flipped, j + 1)
                A(h2g, banks[0][:, :], ACT.Copy).then_inc(h2g_copied, 1)

            def item(i):
                act.wait_ge(gate_clamped, i + 1)
                A(sbuf_, gbuf, ACT.Sigmoid, scale=ALPHA).then_inc(swish_ready, 1)
                act.wait_ge(selw_flipped, i + 1)
                A(SelWT, banks[5][:, 0:T], ACT.Copy).then_inc(selw_copied, 1)
                act.wait_ge(act_flipped, i + 1)
                A(actT, banks[3][:, :], ACT.Copy).then_inc(act_copied, 1)
                copy_gathered(i + 1)
                copy_flipped(i + 1)
                act.wait_ge(dn_ready, i + 1)
                A(dng, banks[4][:, :], ACT.Copy).then_inc(dn_copied, 1)

            wait_taken(act, TURN["xitems"])
            count = act.value_load(itemtab[0:1, NI:NI + 1], min_val=0, max_val=MAXEXTRA) + E
            copy_gathered(0)
            copy_flipped(0)
            item(0)
            with act.Fori(1, count) as i:
                item(i)
            act.wait_ge(summed, count * 8 + 2)
            A(hT[:, :, :], xT[:, :, :], ACT.Square).then_inc(x3sq_ready, 1)
            act.wait_ge(root3_wanted, 1)
            A(small[:, 0:T], small[:, 0:T], ACT.Sqrt).then_inc(root3_ready, 1)

        @block.vector
        def _(dve):
            S = Steps(dve, vector_step)
            step = S.then_wait
            TT, TS, STT = nc.vector.tensor_tensor, nc.vector.tensor_scalar, nc.vector.scalar_tensor_tensor
            nc.vector.memset(ones[:, :], 1.0).then_inc(ones_set, 1)
            step(nc.vector.memset(cpad, 0.0))
            nc.vector.memset(vtok[64:128, 2, :], 0.0)
            nc.vector.memset(attT[64:128, :, TP:T], 0.0).then_inc(pads_set, 1)
            dve.wait_ge(csig_ready, 1)
            TT(cpad[:, :, 0:NROW], cT, csig, ALU.mult).then_inc(cond_ready, 1)
            dve.wait_ge(consts_landed, 32)
            lb2 = V("lb").rearrange("p (l h) -> p l h", l=2)
            step(TT(lbt[:, 2, :], lb2[:, 0, :], lb2[:, 1, :], ALU.max))
            TT(lbt[:, 0:2, :], lb2, lbt[:, 2:3, :].broadcast_to([P, 2, H]), ALU.subtract).then_inc(lbexp_wanted, 1)
            for i in range(3):
                wait_filled(dve, f"adaT{i}")
                v = bank_of(f"adaT{i}")[:, :].rearrange("p (j g r) -> p j g r", j=4, g=4)[:, :, :, 0:NROW]
                o = modT[:, 16 * i:16 * i + 16, :].rearrange("p (g j) r -> p j g r", j=4)
                bias = V("ada_b")[:, 16 * i:16 * i + 16].rearrange("p (g j) -> p j g", j=4).unsqueeze(3)\
                    .broadcast_to([P, 4, 4, NROW])
                TT(o, v, bias, ALU.add).then_inc(taken["v"], 1)
            dve.wait_ge(lbexp_ready, 1)
            step(TT(lbt[:, 2, :], lbt[:, 0, :], lbt[:, 1, :], ALU.add))
            step(nc.vector.reciprocal(lbt[:, 2, :], lbt[:, 2, :]))
            step(TT(lbt[:, 0, :], lbt[:, 0, :], lbt[:, 2, :], ALU.mult))
            step(TS(lbt[:, 1, :], lbt[:, 0, :], -1.0, 1.0, ALU.mult, ALU.add))
            dve.wait_ge(taken["v"], taken_count(TURN["adaT2"]))
            for at, name in ((8, "norm1"), (32, "norm2")):
                step(STT(modT[:, at:at + 8, :], modT[:, at:at + 8, :], 1.0,
                         V(name).unsqueeze(2).broadcast_to([P, 8, NROW]), ALU.add, ALU.mult))

            def inverse_rms(src, dst, n, wanted, ready, value, sem_taken):
                ins = TS(dst, src, 1.0 / n, EPS, ALU.mult, ALU.add)
                if sem_taken is not None:
                    step(ins)
                    TS(dst, dst, 1.0, None, ALU.mult).then_inc(wanted, 1)
                else:
                    ins.then_inc(wanted, 1)
                dve.wait_ge(ready, value)
                step(nc.vector.reciprocal(dst, dst))

            def modulate(gain, shift):
                def s(ap):
                    return ap.rearrange("p c (b t) -> p c b t", t=TSQ)
                hp, hs = hT[:, :, 0:TP], s(hT[:, :, TP:T])
                mg, msh = modT[:, gain:gain + 8, :], modT[:, shift:shift + 8, :]
                bp = lambda m: m[:, :, 0:1].broadcast_to([P, 8, TP])
                bs = lambda m: m[:, :, 1:NROW].unsqueeze(3).broadcast_to([P, 8, NSEQ, TSQ])
                TT(hp, hp, bp(mg), ALU.mult)
                step(TT(hs, hs, bs(mg), ALU.mult))
                TT(hp, hp, bp(msh), ALU.add)
                return TT(hs, hs, bs(msh), ALU.add)

            def spread(row):
                return row.unsqueeze(1).broadcast_to([P, DC, T])

            r0 = small[:, 0:T]
            wait_filled(dve, "ss1")
            TS(r0, bank_of("ss1")[:, 0:T], 1.0 / D, EPS, ALU.mult, ALU.add).then_inc(taken["v"], 1)
            dve.wait_ge(root_ready, 1)
            step(nc.vector.reciprocal(r0, r0))
            step(TT(hT[:, :, :], xT[:, :, :], spread(r0), ALU.mult))
            modulate(8, 0).then_inc(h_ready, 1)

            scratch = [0]

            def gated(name, dst, factor):
                m = scratch[0]
                dve.wait_ge(sig_ready, m + 1)
                STT(dst, bank_of(name)[:, 0:T], factor, small[:, (m % 2) * T:(m % 2 + 1) * T], ALU.mult, ALU.mult)\
                    .then_inc(taken["v"], 1)
                scratch[0] += 1

            o = br[0]
            for u in range(4):
                gated(f"hq{u}", o["q"][:, u, :], float(P) ** -0.5)
            dve.wait_ge(taken["s"], taken_count(TURN["hf3"]))
            for u in range(4):
                ins = TS(o["D"][:, u, :], o["k"][:, u, :], lbt[:, 1, u:u + 1], lbt[:, 0, u:u + 1], ALU.mult, ALU.add)
            step(ins)
            TS(o["k"], o["D"], -1.0, 1.0, ALU.mult, ALU.add).then_inc(exp_wanted, 1)

            def branch_operands(bi):
                o = br[bi]
                n = o["n"]
                got = [5 if bi else 1]

                def wait_exp():
                    got[0] += 1
                    dve.wait_ge(exp_ready, got[0])

                if bi == 0:
                    dve.wait_ge(exp_wanted, 1)
                    dve.wait_ge(exp_ready, 1)
                for u in range(n):
                    ins = nc.vector.tensor_tensor_scan(o["B"][:, u, :], C("carry"), o["D"][:, u, :], 0.0, ALU.mult, ALU.add)
                step(ins)

                def parts(ap):
                    return [ap[:, :, 0:TP].rearrange("p u (c t) -> p u c t", t=CH),
                            ap[:, :, TP:T].rearrange("p u (c t) -> p u c t", t=TSQ)]
                Bp, Dp = parts(o["B"]), parts(o["D"])

                def against(pos, flip):
                    for x, (b, d, t) in enumerate(zip(Bp, Dp, (CH, TSQ))):
                        at = (t - 1) if pos == "last" else t // 2 - 1
                        ref = b[:, :, :, at:at + 1].broadcast_to([P, n, NCH, t])
                        ins = TT(d, ref, b, ALU.subtract) if flip else TT(d, b, ref, ALU.subtract)
                    return ins

                against("last", True).then_inc(exp_wanted, 1)
                wait_exp()
                step(TT(o["kd"], o["k"], o["D"], ALU.mult))
                step(against("mid", False))
                TS(o["D"], o["D"], -CLAMP, CLAMP, ALU.max, ALU.min).then_inc(exp_wanted, 1)
                wait_exp()
                step(TT(o["qs"], o["q"], o["qs"], ALU.mult))
                wait_exp()
                TT(o["k"], o["k"], o["D"], ALU.mult).then_inc(exp_wanted, 1)
                wait_exp()
                TT(o["q"], o["q"], o["D"], ALU.mult).then_inc(ops_ready, 1)

            branch_operands(0)
            for h in range(4):
                gated(f"hg{h}", gates[:, h, :], V("hgain"))
            g = br[1]
            for u in range(2):
                wait_filled(dve, f"gq{u}")
                TS(g["q"][:, u, :], bank_of(f"gq{u}")[:, 0:T], 64.0 ** -0.5, None, ALU.mult).then_inc(taken["v"], 1)
            for u in range(2):
                wait_filled(dve, f"gk{u}")
                TS(g["k"][:, u, :], bank_of(f"gk{u}")[:, 0:T], 1.0, None, ALU.mult).then_inc(taken["v"], 1)
            wait_filled(dve, "gr")
            TS(grT, bank_of("gr")[0:RANK, 0:T], 1.0, None, ALU.mult).then_inc(taken["v"], 1)
            for h in range(4):
                gated(f"gg{h}", gates[:, 4 + h, :], V("ggain"))
            small2 = small[:, :].rearrange("p (u t) -> p u t", u=2)
            dve.wait_ge(taken["v"], taken_count(TURN["gg3"]))
            for u in range(2):
                wait_filled(dve, f"low{u}")
                TS(g["D"][:, u, :], bank_of(f"low{u}")[:, 0:T], V("gla_b")[:, u:u + 1], None, ALU.add)
                TS(small2[:, u, :], bank_of(f"low{u}")[:, 0:T], V("gla_b")[:, u:u + 1], 0.0, ALU.add, ALU.min)\
                    .then_inc(taken["v"], 1)
            dve.wait_ge(taken["v"], taken_count(TURN["low1"]))
            STT(g["D"], small2, 2.0, g["D"], ALU.mult, ALU.subtract).then_inc(low_wanted, 1)
            dve.wait_ge(low_ready, 1)
            dve.wait_ge(taken["v"], taken_count(TURN["low1"]))
            step(TT(g["D"], small2, g["D"], ALU.subtract))
            step(TS(g["D"], g["D"], 1.0 / GATE_NORM, None, ALU.mult))

            def recurrence(bi):
                for ui, (b, u) in enumerate(UNITS):
                    if b != bi:
                        continue
                    o = br[b]
                    heads = [h for h in HEADS if h[0] == b and h[1] == u]
                    for (_, _, hh, n, p0, dk) in heads:
                        dve.wait_ge(att_ready, n + 1)
                        if n:
                            dve.wait_ge(o_ready, n - hh)
                        TT(attT[:, hh, 0:TP].rearrange("p (a t) -> p a t", a=2), banks[0][:, 0:TP].rearrange("p (a t) -> p a t", a=2),
                           C("mask_prompt").unsqueeze(1).broadcast_to([P, 2, P]), ALU.mult)
                        TT(attT[0:64, hh, TP:T], banks[0][0:64, TP:T], C("mask_sample", 64), ALU.mult).then_inc(att_masked, 1)
                    dve.wait_ge(u_ready, ui + 1)
                    if ui:
                        dve.wait_ge(prompt_state_out, [0, 16, 32, 48, 64, 96][ui])
                    step(TS(Sst[:, 0, :], banks[3][:, 0:P], 1.0, None, ALU.mult))
                    for c in range(1, NCH):
                        ins = STT(Sst[:, c, :], Sst[:, c - 1, :], o["D"][:, u, c * CH + CH - 1:c * CH + CH],
                                  banks[3 + c % 4][:, (c // 4) * P:(c // 4 + 1) * P], ALU.mult, ALU.add)
                        if c < NCH - 1:
                            step(ins)
                    ins.then_inc(chain_done, 1)
                    for (_, _, hh, n, p0, dk) in heads:
                        dve.wait_ge(o_squared, n + 1)
                        TT(gates[:, n, :], gates[:, n, :], banks[2][:, 0:T], ALU.mult).then_inc(o_gated, 1)
                        dve.wait_ge(su_ready, n + 1)
                        for s in range(NSEQ):
                            t1 = TP + s * TSQ + TSQ - 1
                            st = S0[p0:p0 + dk, ui % 2, s, :]
                            ins = STT(st, st, o["D"][p0:p0 + dk, u, t1:t1 + 1],
                                      banks[3 + s // 4][p0:p0 + dk, (s % 4) * P:(s % 4 + 1) * P], ALU.mult, ALU.add)
                        ins.then_inc(su_added, 1)

            recurrence(0)
            branch_operands(1)
            recurrence(1)
            r8 = small[0:8, 0:T]
            dve.wait_ge(o_summed, 8)
            TS(r8, banks[7][0:8, 0:T], 1.0 / P, EPS, ALU.mult, ALU.add).then_inc(root_wanted, 1)
            dve.wait_ge(root_ready, 2)
            nc.vector.reciprocal(r8, r8).then_inc(norms_done, 1)
            for n in range(8):
                wait_filled(dve, f"nrm{n}")
                TT(gates[:, n, :], gates[:, n, :], bank_of(f"nrm{n}")[:, 0:T], ALU.mult).then_inc(taken["v"], 1)
            dve.wait_ge(taken["s"], taken_count(TURN["mb7"]))
            for f in range(DC):
                wait_filled(dve, f"bh{f}")
                TT(merged[:, f, :], ma[:, f, :], bank_of(f"bh{f}")[:, 0:T], ALU.mult).then_inc(taken["v"], 1)
            for f in range(DC):
                wait_filled(dve, f"bg{f}")
                TT(mb[:, f, :], mb[:, f, :], bank_of(f"bg{f}")[:, 0:T], ALU.mult).then_inc(taken["v"], 1)
            dve.wait_ge(taken["v"], taken_count(TURN["bg7"]))
            TT(merged, merged, mb, ALU.add).then_inc(merged_done, 1)
            for f in range(DC):
                wait_filled(dve, f"out{f}")
                b = bank_of(f"out{f}")
                step(TT(small[:, 0:TP // 4].rearrange("p (b t) -> p b t", t=TSQ), b[:, TP:T].rearrange("p (b t) -> p b t", t=TSQ),
                        modT[:, 16 + f, 1:NROW].unsqueeze(2).broadcast_to([P, NSEQ, TSQ]), ALU.mult))
                STT(xT[:, f, 0:TP], b[:, 0:TP], modT[:, 16 + f, 0:1], xT[:, f, 0:TP], ALU.mult, ALU.add).then_inc(taken["v"], 1)
                ins = TT(xT[:, f, TP:T], xT[:, f, TP:T], small[:, 0:TP // 4], ALU.add)
                if f < DC - 1:
                    step(ins)
            ins.then_inc(merged_done, 1)
            wait_filled(dve, "ss2")
            TS(r0, bank_of("ss2")[:, 0:T], 1.0 / D, EPS, ALU.mult, ALU.add).then_inc(taken["v"], 1)
            dve.wait_ge(root_ready, 3)
            step(nc.vector.reciprocal(r0, r0))
            step(TT(hT[:, :, :], xT[:, :, :], spread(r0), ALU.mult))
            modulate(32, 24).then_inc(h2_ready, 1)

            step(nc.vector.memset(Lg[64:128, 2, :], 0.0))
            wait_filled(dve, "logits")
            b = bank_of("logits")
            TS(Lg[:, 0:2, :], b[:, 0:2 * E].rearrange("p (a e) -> p a e", a=2), 1.0, None, ALU.mult)
            TS(Lg[0:64, 2, :], b[0:64, 2 * E:3 * E], 1.0, None, ALU.mult).then_inc(taken["v"], 1)
            dve.wait_ge(taken["v"], taken_count(TURN["logits"]))
            for p in range(3):
                ins = nc.vector.max(top8[:, p, :], Lg[:, p, :])
            step(ins)
            be = lambda m: m.broadcast_to([P, 3, E])
            v1, v4 = top8[:, :, 0:1], top8[:, :, TOPK - 1:TOPK]
            TT(comb, Lg, be(v1), ALU.subtract).then_inc(rexp_wanted, 1)
            TT(sel, Lg, be(v4), ALU.is_gt)
            step(TT(eqm, Lg, be(v4), ALU.is_equal))
            step(nc.vector.tensor_reduce(ngt, sel, AX, ALU.add))
            step(TS(ngt, ngt, -1.0, TOPK + 0.5, ALU.mult, ALU.add))
            for p in range(3):
                ins = nc.vector.tensor_tensor_scan(cum[:, p, :], ones[:, 0:E], eqm[:, p, :], 0.0, ALU.mult, ALU.add)
            step(ins)
            step(TT(cum, cum, be(ngt), ALU.is_lt))
            step(TT(eqm, eqm, cum, ALU.mult))
            step(TT(sel, sel, eqm, ALU.add))
            step(nc.vector.memset(sel[64:128, 2, :], 0.0))
            for p in range(3):
                ins = TT(selx[:, p, :].rearrange("p (e k) -> p e k", k=P // E), sel[:, p, :].unsqueeze(2).broadcast_to([P, E, P // E]),
                         ones[:, :].rearrange("p (e k) -> p e k", k=P // E), ALU.mult)
            ins.then_inc(sel_routed, 1)
            dve.wait_ge(rexp_ready, 1)
            step(TT(comb, comb, sel, ALU.mult))
            step(nc.vector.tensor_reduce(tot, comb, AX, ALU.add))
            step(nc.vector.tensor_scalar(tot, tot, 1e-30, None, ALU.max))
            step(nc.vector.reciprocal(tot, tot))
            step(TT(comb, comb, be(tot), ALU.mult))
            wait_filled(dve, "rank")
            TS(posm, bank_of("rank")[:, 0:3 * E].rearrange("p (a e) -> p a e", a=3), 1.0, None, ALU.add).then_inc(taken["v"], 1)
            dve.wait_ge(taken["v"], taken_count(TURN["rank"]))
            step(TT(posm, posm, sel, ALU.mult))
            TS(posm, posm, -1.0, None, ALU.add).then_inc(comb_ready, 1)
            wait_filled(dve, "count")
            TS(flag[:, 0, :], bank_of("count")[:, 0:1], C("thr"), None, ALU.is_gt).then_inc(taken["v"], 1)
            TT(thrrep[:, 0, :], C("thr").broadcast_to([P, P]), ones[:, :], ALU.mult).then_inc(thr_ready, 1)
            wait_filled(dve, "place")
            dve.wait_ge(taken["v"], taken_count(TURN["count"]))
            b = bank_of("place")
            step(TS(slotq[:, 0, :], b[:, 0:1], 1.0, None, ALU.mult))
            TS(itemtab[0:1, NI:NI + 1], b[0:1, 1:2], 1.0, None, ALU.mult).then_inc(taken["v"], 1)
            TS(Oq[:, 0, :], C("item_no"), slotq[:, 0, :], flag[:, 0, :], ALU.is_equal, ALU.mult).then_inc(oq_ready, 1)
            for name, dst in (("posT", posT), ("combT", combT)):
                wait_filled(dve, name)
                TS(dst, bank_of(name)[0:E, 0:T], 1.0, None, ALU.mult).then_inc(taken["v"], 1)
            dve.wait_ge(comb_ready, 1)
            TS(posI[:, :, 0:E], posm, 1.0, None, ALU.mult)
            TS(wI[:, :, 0:E], comb, 1.0, None, ALU.mult)
            step(nc.vector.memset(posI[64:128, 2, E:NI], -1.0))
            step(nc.vector.memset(wI[64:128, 2, E:NI], 0.0))
            TS(OHI[0:96, 0:E], C("own96", 96), 1.0, None, ALU.mult)
            TS(itemtab[0:1, 0:E], C("items0", 1), 1.0, None, ALU.mult)
            X = MAXEXTRA + 1
            wait_filled(dve, "xitems")
            b = bank_of("xitems")
            TS(OHI[0:96, E:NI], b[0:96, 0:X], 1.0, None, ALU.mult).then_inc(xoh_ready, 1)
            step(TS(itemtab[0:1, E:NI], b[0:1, 32:32 + X], 1.0, None, ALU.mult))
            TS(frow[:, 0, :], b[:, 64:64 + X], 1.0, None, ALU.mult).then_inc(taken["v"], 1)
            wait_filled(dve, "xpos")
            dve.wait_ge(taken["v"], taken_count(TURN["xitems"]))
            b = bank_of("xpos")
            TT(posI[:, 0:2, E:NI], b[:, 0:2 * X].rearrange("p (a i) -> p a i", a=2), frow.broadcast_to([P, 2, X]), ALU.subtract)
            TT(posI[0:64, 2, E:NI], b[0:64, 2 * X:3 * X], frow[0:64, 0, :], ALU.subtract).then_inc(taken["v"], 1)
            wait_filled(dve, "xcomb")
            b = bank_of("xcomb")
            TS(wI[:, 0:2, E:NI], b[:, 0:2 * X].rearrange("p (a i) -> p a i", a=2), 1.0, None, ALU.mult)
            TS(wI[0:64, 2, E:NI], b[0:64, 2 * X:3 * X], 1.0, None, ALU.mult).then_inc(taken["v"], 1)
            dve.wait_ge(bgu_landed, 48)
            step(TS(bgu[0:96, :], bguf, 1.0, None, ALU.mult))
            step(TT(bguf, bguf, bgu[0:96, :], ALU.subtract))
            TS(bgu[32:64, :], bguf[32:64, :], 1.0, None, ALU.mult)
            step(TS(bgu[64:96, :], bguf[64:96, :], 1.0, None, ALU.mult))
            step(TT(bguf[64:96, :], bguf[64:96, :], bgu[64:96, :], ALU.subtract))
            step(TS(bgu[64:96, :], bguf[64:96, :], 1.0, None, ALU.mult))
            for f in range(DC):
                wait_filled(dve, f"bdn{f}")
                TS(yacc[:, f, TP:T], bank_of(f"bdn{f}")[:, TP:T], 1.0, None, ALU.mult).then_inc(summed, 1) if f == DC - 1 else \
                    TS(yacc[:, f, TP:T], bank_of(f"bdn{f}")[:, TP:T], 1.0, None, ALU.mult)
                TS(yacc[:, f, 0:TP], bank_of(f"bdn{f}")[:, 0:TP], 1.0, None, ALU.mult).then_inc(taken["v"], 1)
            dve.wait_ge(taken["v"], taken_count(len(TURNS) - 1))

            def col(tab, p, j):
                return tab[:, p, j:j + 1] if isinstance(j, int) else tab[:, p, ds(j, 1)]

            def select(j):
                for p in range(3):
                    ins = TS(Sel[:, p, :], C("slot_no")[:, 0:CAP], col(posI, p, j), None, ALU.is_equal)
                ins.then_inc(sel_ready, 1)

            def select_bias(j):
                c = OHI[0:96, j:j + 1] if isinstance(j, int) else OHI[0:96, ds(j, 1)]
                TS(bsel[0:96, :], ones[0:96, 0:CAP], c, None, ALU.mult).then_inc(bsel_ready, 1)

            def add_scattered(i):
                dve.wait_ge(summed, i * 8 + 1)
                for q in range(4):
                    for h in range(2):
                        n = 2 * q + h
                        dve.wait_ge(scattered, i * 8 + (n + 1))
                        f = 4 * h + q
                        TT(yacc[:, f, :], yacc[:, f, :], banks[SCATTER[n]][:, 0:T], ALU.add).then_inc(summed, 1)

            def item(i, first):
                dve.wait_ge(gathered, i + 1)
                select(i + 1)
                if not first:
                    dve.wait_ge(selw_flipped, i)
                for p in range(3):
                    ins = TS(SelW[:, p, :], C("slot_no"), col(posI, p, i), col(wI, p, i), ALU.is_equal, ALU.mult)
                ins.then_inc(selw_ready, 1)
                dve.wait_ge(gate_ready, i + 1)
                TS(gbuf, banks[1][:, :], LIMIT, None, ALU.min).then_inc(gate_clamped, 1)
                dve.wait_ge(up_ready, i + 1)
                if not first:
                    dve.wait_ge(act_ready, i)
                step(TS(ubuf, banks[2][:, :], -LIMIT, LIMIT, ALU.max, ALU.min))
                step(STT(ubuf, ubuf, 1.0, gbuf, ALU.add, ALU.mult))
                dve.wait_ge(swish_ready, i + 1)
                TT(actb, ubuf, sbuf_, ALU.mult).then_inc(act_ready, 1)
                select_bias(i + 1)
                if not first:
                    add_scattered(i - 1)

            PER_ITEM = 2
            select(0)
            select_bias(0)
            item(0, True)
            n0 = S.n
            count = dve.value_load(itemtab[0:1, NI:NI + 1], min_val=0, max_val=MAXEXTRA) + E
            with dve.Fori(1, count) as i:
                S.base = (i - 1) * PER_ITEM
                item(i, False)
                assert S.n == n0 + PER_ITEM
            add_scattered(count - 1)
            S.base = (count - 2) * PER_ITEM
            dve.wait_ge(summed, count * 8 + 1)

            def samples(ap):
                return ap.rearrange("p c (b t) -> p c b t", t=TSQ)
            TT(yacc[:, :, 0:TP], yacc[:, :, 0:TP], modT[:, 40:48, 0:1].broadcast_to([P, DC, TP]), ALU.mult)
            step(TT(samples(yacc[:, :, TP:T]), samples(yacc[:, :, TP:T]),
                    modT[:, 40:48, 1:NROW].unsqueeze(3).broadcast_to([P, DC, NSEQ, TSQ]), ALU.mult))
            TT(xT[:, :, :], xT[:, :, :], yacc[:, :, :], ALU.add).then_inc(summed, 1)
            dve.wait_ge(ss3_ready, 1)
            TS(r0, banks[0][:, 0:T], 1.0 / D, EPS, ALU.mult, ALU.add).then_inc(root3_wanted, 1)
            dve.wait_ge(root3_ready, 1)
            step(nc.vector.reciprocal(r0, r0))
            step(TT(xT[:, :, :], xT[:, :, :], spread(r0), ALU.mult))
            TT(xT[:, :, :], xT[:, :, :], V("final").unsqueeze(2).broadcast_to([P, DC, T]), ALU.mult).then_inc(y_ready, 1)


def kernel(**inputs):
    import numpy as _np
    import concourse.bacc as _bacc
    from concourse import mybir as _mybir
    from concourse.bass_utils import run_bass_kernel_spmd as _run

    def fm(v):
        return _np.asarray(v).reshape(-1, P).T

    g = {k: _np.asarray(v) for k, v in inputs.items()}
    x = _np.concatenate([g["x_prompt"].reshape(TP, D), g["x_sample"].reshape(NSEQ * TSQ, D)])
    c = _np.concatenate([g["c_prompt"], g["c_sample"]])
    vec = _np.concatenate([fm(g["ada_b"][0]), fm(g["norm1_g"][0]), fm(g["norm2_g"][0]), fm(g["final_g"]),
                           fm(g["hgrn_lb"].reshape(-1)), fm(g["hgrn_norm_g"][0]), fm(g["gla_norm_g"][0]),
                           fm(g["gla_gate_b"][0])], 1)
    arrays = {
        "xT": x.reshape(T, DC, P).transpose(2, 1, 0),
        "cT": c.reshape(NROW, DC, P).transpose(2, 1, 0),
        "vec": vec,
        "consts": CONSTS,
        "gla_w2": g["gla_gate_w2"][0],
        "router_w": g["router_w"][0].reshape(DC, P, E).transpose(1, 0, 2),
        "router_b": g["router_b"],
    }
    for name in ("state_hgrn", "state_gla", "ada_w", "w_in", "w_branch_h", "w_branch_g", "w_out",
                 "exp_w_gu", "exp_b_gu", "exp_w_dn", "exp_b_dn"):
        arrays[name] = g[name]
    arrays = {k: _np.ascontiguousarray(v) for k, v in arrays.items()}
    outs = {"yT": (P, DC, T), "hgrn_prompt": (1, 1, H, 128, 128), "gla_prompt": (1, 1, H, 64, 128),
            "hgrn_sample": (1, NSEQ, H, 128, 128), "gla_sample": (1, NSEQ, H, 64, 128)}
    nc = _bacc.Bacc("TRN2", target_bir_lowering=False, num_devices=1)
    aps = {k: nc.dram_tensor(f"in_{k}", v.shape, _mybir.dt.from_np(v.dtype), kind="ExternalInput").ap()
           for k, v in arrays.items()}
    for k, s in outs.items():
        aps[k] = nc.dram_tensor(f"out_{k}", s, _mybir.dt.float32, kind="ExternalOutput").ap()
    build(nc, aps)
    r = _run(nc, [{f"in_{k}": v for k, v in arrays.items()}], core_ids=[0]).results[0]
    y = r["out_yT"].transpose(2, 1, 0).reshape(T, D)
    return (y[:TP].reshape(1, TP, D), y[TP:].reshape(NSEQ, TSQ, D), r["out_hgrn_prompt"], r["out_gla_prompt"],
            r["out_hgrn_sample"], r["out_gla_sample"])
```

```python
from contextlib import ExitStack

import numpy as np
import concourse.bass as bass
from concourse import mybir

F32 = mybir.dt.float32
BF16 = mybir.dt.bfloat16
I32 = mybir.dt.int32
ACT = mybir.ActivationFunctionType
ALU = mybir.AluOpType
AX = mybir.AxisListType.X
ds = bass.ds

P = 128
D = 1024
DC = D // P
TP, NSEQ, TSQ = 256, 8, 8
T = TP + NSEQ * TSQ
TILES = [(0, 128), (128, 128), (256, 64)]
NROW = 1 + NSEQ
H = 4
RANK = 16
E = 32
TOPK = 4
CAP = 64
CH = 32
NCH = TP // CH
MAXEXTRA = TOPK * T // CAP
NI = E + MAXEXTRA + 1
EPS = 1e-6
LIMIT, ALPHA = 7.0, 1.702
GATE_NORM = 16.0
CLAMP = 40.0
NSLOT, SLOT = 12, 2048
REC_BANKS = (0, 1, 2, 3, 4)

CONST_COLS = {}


def _constants():
    cols = []

    def put(name, a):
        b = np.zeros((P, a.shape[1]), np.float32)
        b[:a.shape[0]] = a
        CONST_COLS[name] = (sum(c.shape[1] for c in cols), a.shape[1])
        cols.append(b)

    i = np.arange(P)
    put("ident", np.eye(P))
    put("before", (i[:, None] < i[None, :]).astype(np.float32))
    put("mask_prompt", ((i[:, None] <= i[None, :]) & (i[:, None] // CH == i[None, :] // CH)).astype(np.float32))
    j = np.arange(NSEQ * TSQ)
    put("mask_sample", ((j[:, None] <= j[None, :]) & (j[:, None] // TSQ == j[None, :] // TSQ)).astype(np.float32))
    t = np.arange(T)
    first = np.where(t < TP, t % CH == 0, t % TSQ == 0)
    put("carry", np.tile(np.where(first, 0.0, 1.0), (P, 1)))
    put("seq", (j[:, None] // TSQ % 4 == np.arange(4)[None, :]).astype(np.float32))
    put("chunk", (i[:, None] // CH % 4 == np.arange(4)[None, :]).astype(np.float32))
    put("slot_no", np.tile(np.arange(P) % CAP, (P, 1)))
    per = P // E
    put("thr", (CAP * (i % per + 1))[:, None])
    put("eid", (i // per)[:, None])
    put("pick96", (np.arange(96)[None, :] % E == (i // per)[:, None]).astype(np.float32))
    put("next_eid", (i // per + 1)[:, None])
    put("item_no", np.tile(np.arange(NI), (P, 1)))
    e = np.arange(E)
    put("e_row", e[None, :])
    put("e_col", e[:, None])
    put("before_e", (i[:, None] < per * e[None, :]).astype(np.float32))
    put("upto_e", (i[:, None] < per * (e[None, :] + 1)).astype(np.float32))
    put("own96", (np.arange(96)[None, :] % E == e[:, None]).astype(np.float32))
    put("first96", (np.arange(96) % E == 0)[:, None])
    put("head_col", np.tile((np.arange(16) == 8).astype(np.float32), (P, 1)))
    return np.concatenate(cols, 1)


CONSTS = _constants()
NCONST = CONSTS.shape[1]
VEC = {"ada_b": (0, 48), "norm1": (48, 8), "norm2": (56, 8), "final": (64, 8), "lb": (72, 8),
       "hgain": (80, 1), "ggain": (81, 1), "gla_b": (82, 2)}
NVEC = 84

GROUPS = [
    (0, 1024, [(f"hq{h}", h * 128, 128) for h in range(4)] + [(f"hf{h}", 512 + h * 128, 128) for h in range(4)]),
    (1024, 1024, [(f"hi{p}", 0, 512) for p in range(3)] + [(f"hg{h}", 512 + h * 128, 128) for h in range(4)]),
    (2048, 1024, [(f"gq{u}", u * 128, 128) for u in range(2)] + [(f"gk{u}", 256 + u * 128, 128) for u in range(2)]
     + [(f"gv{p}", 512, 512) for p in range(3)]),
    (3072, 528, [("gr", 0, 16)] + [(f"gg{h}", 16 + h * 128, 128) for h in range(4)]),
    (3600, 1024, [(f"ma{f}", f * 128, 128) for f in range(8)]),
    (4624, 1024, [(f"mb{f}", f * 128, 128) for f in range(8)]),
]
FILL = {(0, "a"): ["gq0"], (0, "b"): ["gq1"], (0, "c0"): ["gk0"],
        (1, "a"): ["gk1"], (1, "b"): ["gv0"], (1, "c0"): ["gv1"],
        (2, "a"): ["gv2"], (2, "b"): ["gr", "gg0"], (2, "c0"): ["gg1"],
        (3, "a"): ["gg2"], (3, "b"): ["gg3"], (3, "c0"): ["low0", "low1"],
        (4, "u"): ["mb0"], (4, "b"): ["mb1"], (4, "c0"): ["mb2"],
        (5, "u"): ["mb3"], (5, "b"): ["mb4"], (5, "c0"): ["mb5"]}


def _turns():
    def owned(names):
        return [(n, "s" if n[:2] in ("hi", "gv", "hf", "ma", "mb", "to") or n[:-1] == "ada" else "v") for n in names]

    def blocks(g):
        return [b[0] for b in GROUPS[g][2]]

    first = ["ss1", "ada0", "adaT0"] + blocks(0) + ["ada1"] + blocks(1) + ["adaT1", "ada2", "adaT2"]
    out = [(n, o, (6 - (len(first) - 1 - i)) % 7) for i, (n, o) in enumerate(owned(first))]
    out += [(n, o, 5 + i % 2) for i, (n, o) in enumerate(owned(sum((FILL[k] for k in FILL if k[0] < 4), [])))]
    out += [(n, o, bank) for (n, o), bank in zip(owned(blocks(4)), (5, 6, 0, 1, 2, 3, 5, 6))]
    out += [(n, o, 5 + i % 2) for i, (n, o) in enumerate(owned(sum((FILL[k] for k in FILL if k[0] >= 4), [])))]
    rest = (["mb6", "mb7"] + [f"nrm{n}" for n in range(8)] + [f"bh{f}" for f in range(8)] + [f"bg{f}" for f in range(8)]
            + [f"out{f}" for f in range(8)] + ["ss2", "logits", "lflip"] + [f"tok{p}{q}" for p in range(3) for q in range(2)]
            + ["rank"])
    out += [(n, o, (5 + i) % 7) for i, (n, o) in enumerate(owned(rest))]
    out += list(zip(("count", "place", "posT", "combT", "xitems", "xpos", "xcomb"), "vvvvvvv", (3, 4, 5, 6, 3, 4, 5)))
    return out


TURNS = _turns()
TURN = {name: n for n, (name, _, _) in enumerate(TURNS)}


def taken_count(n):
    return sum(1 for _, o, _ in TURNS[:n + 1] if o == TURNS[n][1])


def slot_plan():
    plan, used = [], 0
    last = [g[2][-1][0] for g in GROUPS]
    groups = ([("ada0", 8), (last[0], 4), ("ada1", 8), (last[1], 4), ("ada2", 8)] + [(n, 4) for n in last[2:]]
              + [("bh7", 2), ("bg7", 2), ("out7", 4)])
    for turn, n in groups:
        for s in range(n):
            if s < n - 1:
                used += 1
                plan.append(("used", used))
            else:
                plan.append(("turn", TURN[turn] + 1))
    return plan, used


PLAN, USED0 = slot_plan()
NPRE = len(PLAN)
GROUP_SLOT = [8, 20, 32, 36, 40, 44]
IT_SLOTS = 12
SLOT0 = NPRE % NSLOT


def build(nc, a):
    ctx = ExitStack()
    with ctx:
        def sb(name, shape, dt=F32):
            return ctx.enter_context(nc.sbuf_tensor(name, shape, dt))

        def sem(name):
            return ctx.enter_context(nc.semaphore(name))

        ring = sb("ring", [P, NSLOT, SLOT])
        xT = sb("xT", [P, DC, T])
        hT = sb("hT", [P, DC, T])
        vtok = sb("vtok", [P, 3, D])
        gates = sb("gates", [P, 2 * H, T])
        big = sb("big", [P, 6 * H * T])
        gla = sb("gla", [P, 3, 2, T])
        consts = sb("consts", [P, NCONST])
        vec = sb("vec", [P, NVEC])
        modT = sb("modT", [P, 48, NROW])
        small = sb("small", [P, 2 * T])
        kdtok = sb("kdtok", [P, 3, P])
        attT = sb("attT", [P, 2, T])
        Sst = sb("Sst", [P, NCH, P])
        S0 = sb("S0", [P, 2, NSEQ, P])
        vblk = sb("vblk", [64, 4, P])
        grT = sb("grT", [RANK, T])
        w2 = sb("w2", [RANK, 2 * P])
        osq = sb("osq", [P, T])
        ones = sb("ones", [P, P])
        itemtab = sb("itemtab", [1, NI + 1 + E], I32)
        lbt = sb("lbt", [P, 3, H])

        cT = Sst[:, 0:1, :].rearrange("p a b -> p (a b)")[:, 0:DC * NROW].rearrange("p (c r) -> p c r", c=DC)
        csig = Sst[:, 1:2, :].rearrange("p a b -> p (a b)")[:, 0:DC * NROW].rearrange("p (c r) -> p c r", c=DC)
        cpad = Sst[:, 2:4, :].rearrange("p a b -> p (a b)").rearrange("p (c r) -> p c r", c=DC)
        modsb = gates[:, 4:6, :].rearrange("p a b -> p (a b)")[:, 0:512]
        rw = Sst[:, 0:2, :].rearrange("p a b -> p (a b)").rearrange("p (c e) -> p c e", c=DC)
        rb = Sst[0:E, 2, 0:1]
        bdn = S0[0:E, 0, :, :].rearrange("p a b -> p (a b)")

        bigv = big[:, :]

        def cut(at, n):
            return bigv[:, at:at + n]

        HT = H * T

        def units(ap, n):
            return ap.rearrange("p (u t) -> p u t", u=n)

        br = [
            dict(n=4, D=units(cut(0, HT), 4), B=units(cut(HT, HT), 4), q=units(cut(2 * HT, HT), 4),
                 k=units(cut(3 * HT, HT), 4), kd=units(cut(4 * HT, HT), 4), qs=units(cut(5 * HT, HT), 4)),
            dict(n=2, D=gla[:, 0, :, :], B=units(cut(0, 2 * T), 2), q=gla[:, 1, :, :], k=gla[:, 2, :, :],
                 kd=units(cut(2 * T, 2 * T), 2), qs=units(cut(4 * T, 2 * T), 2)),
        ]
        vmask = [[cut(6 * T, 4 * P).rearrange("p (c v) -> p c v", c=4), cut(at, 4 * P).rearrange("p (c v) -> p c v", c=4)]
                 for at in (HT, 0)]
        ma = units(cut(4 * HT, 2 * HT), DC)
        mb = units(cut(2 * HT, 2 * HT), DC)
        merged = units(cut(0, 2 * HT), DC)

        def C(name, rows=P):
            at, n = CONST_COLS[name]
            return consts[0:rows, at:at + n]

        def V(name):
            at, n = VEC[name]
            return vec[:, at:at + n]

        off = [0]

        def take(n):
            off[0] += n
            assert off[0] <= 6 * HT
            return cut(off[0] - n, n)

        Sel = take(3 * CAP).rearrange("p (a j) -> p a j", a=3)
        SelW = take(3 * P).rearrange("p (a j) -> p a j", a=3)
        SelWT = take(T)
        gtok = take(512)
        h2g = take(DC * CAP)
        gbuf, ubuf, sbuf_, actb, actT, dng = (take(512) for _ in range(6))
        bgu = take(1024).bitcast(BF16)
        bsel = take(32).bitcast(BF16)
        posI = take(3 * NI).rearrange("p (a i) -> p a i", a=3)
        wI = take(3 * NI).rearrange("p (a i) -> p a i", a=3)
        OHI = take(NI)
        yacc = gates
        h2tok = vtok
        rt = gla[:, :, :, :].rearrange("p a b c -> p (a b c)")
        roff = [0]

        def rtake(n, k=3):
            roff[0] += n * k
            assert roff[0] <= 6 * T
            return rt[:, roff[0] - n * k:roff[0]].rearrange("p (a e) -> p a e", a=k)

        Lg, sel, comb, eqm, cum, posm = (rtake(E) for _ in range(6))
        top8 = rtake(8)
        tot = rtake(1)
        ngt = rtake(1)
        selx = rtake(P)
        flag, slotq = rtake(1, 1), rtake(1, 1)
        Oq = rtake(NI, 1)
        Oe, starts = rtake(NI, 1), rtake(1, 1)
        posT = small[0:E, 0:T]
        combT = small[0:E, T:2 * T]
        logT = combT
        thrrep = rtake(P, 1)
        frow = rtake(NI, 1)
        bguf = cut(2 * HT, 2048)[0:96, :]

        banks = [ctx.enter_context(nc.psum_tensor(f"bank{n}", [P, 512], F32)) for n in range(8)]

        slot_landed = [sem(f"slot_landed{n}") for n in range(NSLOT)]
        slot_used = sem("slot_used")
        turn_filled = sem("turn_filled")
        taken = {"v": sem("turn_taken_by_vector"), "s": sem("turn_taken_by_scalar")}
        x_landed, c_landed, consts_landed, w2_landed = sem("x_landed"), sem("c_landed"), sem("consts_landed"), sem("w2_landed")
        router_landed, bgu_landed, bdn_landed = sem("router_landed"), sem("bgu_landed"), sem("bdn_landed")
        state_landed = [sem("state_landed0"), sem("state_landed1")]
        ones_set, pads_set = sem("ones_set"), sem("pads_set")
        csig_ready, cond_ready = sem("csig_ready"), sem("cond_ready")
        xsq_ready, x2sq_ready, root_wanted, root_ready = sem("xsq_ready"), sem("x2sq_ready"), sem("root_wanted"), sem("root_ready")
        h_ready = sem("h_ready")
        lbexp_wanted, lbexp_ready = sem("lbexp_wanted"), sem("lbexp_ready")
        sig_ready = sem("sig_ready")
        exp_wanted, exp_ready = sem("exp_wanted"), sem("exp_ready")
        ops_ready = sem("ops_ready")
        low_wanted, low_ready = sem("low_wanted"), sem("low_ready")
        kd_flipped, kd_copied = sem("kd_flipped"), sem("kd_copied")
        att_ready, att_masked = sem("att_ready"), sem("att_masked")
        u_ready, chain_done = sem("u_ready"), sem("chain_done")
        o_ready, o_squared, o_summed, o_gated = sem("o_ready"), sem("o_squared"), sem("o_summed"), sem("o_gated")
        vmask_ready, vblk_ready, su_ready, su_added = sem("vmask_ready"), sem("vblk_ready"), sem("su_ready"), sem("su_added")
        prompt_state_out, sample_state_out, y_out = sem("prompt_state_out"), sem("sample_state_out"), sem("y_out")
        norms_done, merged_done, x_updated = sem("norms_done"), sem("merged_done"), sem("x_updated")
        h2_ready, x3_updated = sem("h2_ready"), sem("x3_updated")
        sel_routed, thr_ready, oq_ready, xoh_ready = (sem("sel_routed"), sem("thr_ready"), sem("oq_ready"),
                                                                   sem("xoh_ready"))
        rexp_wanted, rexp_ready = sem("rexp_wanted"), sem("rexp_ready")
        comb_ready = sem("comb_ready")
        sel_ready, gathered, gtok_copied = sem("sel_ready"), sem("gathered"), sem("gtok_copied")
        gtok_flipped, h2g_copied = sem("gtok_flipped"), sem("h2g_copied")
        bsel_ready, gate_ready, up_ready = sem("bsel_ready"), sem("gate_ready"), sem("up_ready")
        gate_clamped, swish_ready, act_ready = sem("gate_clamped"), sem("swish_ready"), sem("act_ready")
        selw_ready, selw_flipped, selw_copied = sem("selw_ready"), sem("selw_flipped"), sem("selw_copied")
        act_flipped, act_copied, dn_ready, dn_copied = sem("act_flipped"), sem("act_copied"), sem("dn_ready"), sem("dn_copied")
        scattered, summed = sem("scattered"), sem("summed")
        x3sq_ready, ss3_ready, root3_wanted, root3_ready, y_ready = (sem("x3sq_ready"), sem("ss3_ready"), sem("root3_wanted"),
                                                                    sem("root3_ready"), sem("y_ready"))
        vector_step, scalar_step = sem("vector_step"), sem("scalar_step")

        block = ctx.enter_context(nc.Block())

        class Steps:

            def __init__(self, eng, sem_):
                self.eng, self.sem, self.n, self.base = eng, sem_, 0, 0

            def then_wait(self, ins):
                ins.then_inc(self.sem, 1)
                self.n += 1
                self.eng.wait_ge(self.sem, self.base + self.n)

        def wait_taken(eng, n):
            owner = TURNS[n][1]
            eng.wait_ge(taken[owner], taken_count(n))

        def bank_of(name):
            return banks[TURNS[TURN[name]][2]]

        def wait_filled(eng, name):
            eng.wait_ge(turn_filled, TURN[name] + 1)

        def landed(eng, n):
            eng.wait_ge(slot_landed[n % NSLOT], 16 * (n // NSLOT + 1))

        def item_slot(s):
            return (SLOT0 + s) % NSLOT

        def item_landed_count(s):
            return 16 * ((NPRE + s) // NSLOT + 1)

        def pair(n):
            return ring[:, n % NSLOT, :].rearrange("p (k c) -> p k c", k=2)

        HEADS = [(0, u, 0, u, 0, 128) for u in range(4)] + [(1, u, hh, 4 + 2 * u + hh, 64 * hh, 64)
                                                             for u in range(2) for hh in range(2)]
        UNITS = [(b, u) for b in range(2) for u in range(br[b]["n"])]
        FIRSTHEAD = [0, 1, 2, 3, 4, 6]
        STATE_DMAS = [1, 1, 2, 2, 4, 4]
        SCATTER = [3, 5, 4, 6, 7, 0, 6, 7]

        @block.sync
        def _(sp):
            n = 0

            def wait_slot(m):
                if m >= NSLOT:
                    kind, val = PLAN[m - NSLOT]
                    sp.wait_ge(slot_used if kind == "used" else turn_filled, val)

            def stream(src, dst):
                nonlocal n
                wait_slot(n)
                sp.dma_start(dst, src).then_inc(slot_landed[n % NSLOT], 16)
                n += 1

            def ada(i):
                for k in range(DC):
                    stream(a["ada_w"][0, k * P:(k + 1) * P, i * SLOT:(i + 1) * SLOT], ring[:, n % NSLOT, :])

            def w_in(gi):
                c0, w, _ = GROUPS[gi]
                assert n == GROUP_SLOT[gi]
                for s in range(4):
                    stream(a["w_in"][0, 2 * s * P:(2 * s + 2) * P, c0:c0 + w].rearrange("(k p) c -> p k c", p=P),
                           pair(n)[:, :, 0:w])

            ada(0)
            w_in(0)
            ada(1)
            w_in(1)
            ada(2)
            for gi in range(2, 6):
                w_in(gi)
            for name, cnt in (("w_branch_h", 2), ("w_branch_g", 2), ("w_out", 4)):
                for s in range(cnt):
                    stream(a[name][0, 2 * s * P:(2 * s + 2) * P, :].rearrange("(k p) c -> p k c", p=P), pair(n))
            assert n == NPRE

            def expert(e, i):
                for s in range(IT_SLOTS):
                    if i is None:
                        wait_slot(NPRE + s)
                    elif s == 7:
                        sp.wait_ge(up_ready, i + 1)
                    elif s == 11:
                        sp.wait_ge(dn_ready, i + 1)
                    else:
                        sp.wait_ge(slot_used, i * 10 + (USED0 + (s if s < 7 else s - 1) + 1))
                    if s < DC:
                        src = a["exp_w_gu"][0, ds(e, 1), s * P:(s + 1) * P, :].rearrange("a p c -> p (a c)")
                        dst = ring[:, item_slot(s), :]
                    else:
                        k = 2 * (s - DC)
                        src = a["exp_w_dn"][0, ds(e, 1), k * P:(k + 2) * P, :].rearrange("a (k p) c -> p (a k) c", p=P)
                        dst = pair(item_slot(s))
                    sp.dma_start(dst, src).then_inc(slot_landed[item_slot(s)], 16)

            expert(0, None)
            wait_taken(sp, TURN["place"])
            with sp.Fori(1, E) as e:
                expert(e, sp.value_load(itemtab[0:1, ds(e + NI, 1)], min_val=0, max_val=NI - 1))
            for x in range(4):
                sp.wait_ge(y_ready, x + 1)
                sp.dma_start(a["yT"][:, 2 * x:2 * x + 2, :], xT[:, 2 * x:2 * x + 2, :]).then_inc(y_out, 16)
            sp.wait_ge(y_out, 64)

        @block.gpsimd
        def _(pool):
            def load_state(ui):
                b, u = UNITS[ui]
                buf = S0[:, ui % 2, :, :]
                if b == 0:
                    src = a["state_hgrn"][0, :, u, :, :].rearrange("b k v -> k b v")
                    pool.dma_start(buf, src).then_inc(state_landed[ui % 2], 16)
                else:
                    for hh in range(2):
                        src = a["state_gla"][0, :, 2 * u + hh, :, :].rearrange("b k v -> k b v")
                        pool.dma_start(buf[64 * hh:64 * hh + 64, :, :], src).then_inc(state_landed[ui % 2], 16)

            pool.dma_start(w2[:, :], a["gla_w2"]).then_inc(w2_landed, 16)
            pool.wait_ge(h_ready, 1)
            load_state(0)
            load_state(1)
            outs_s = [0, 0]
            for ui, (b, u) in enumerate(UNITS):
                pool.wait_ge(chain_done, ui + 1)
                if b == 0:
                    pool.dma_start(a["hgrn_prompt"][0, 0, u, :, :], Sst[:, NCH - 1, :]).then_inc(prompt_state_out, 16)
                else:
                    for hh in range(2):
                        pool.dma_start(a["gla_prompt"][0, 0, 2 * u + hh, :, :],
                                       Sst[64 * hh:64 * hh + 64, NCH - 1, :]).then_inc(prompt_state_out, 16)
                last = FIRSTHEAD[ui + 1] if ui + 1 < len(UNITS) else len(HEADS)
                pool.wait_ge(su_added, last)
                buf = S0[:, ui % 2, :, :]
                if b == 0:
                    pool.dma_start(a["hgrn_sample"][0, :, u, :, :].rearrange("b k v -> k b v"), buf).then_inc(sample_state_out, 16)
                    outs_s[0] += 16
                else:
                    for hh in range(2):
                        pool.dma_start(a["gla_sample"][0, :, 2 * u + hh, :, :].rearrange("b k v -> k b v"),
                                       buf[64 * hh:64 * hh + 64, :, :]).then_inc(sample_state_out, 16)
                        outs_s[0] += 16
                if ui + 2 < len(UNITS):
                    pool.wait_ge(sample_state_out, outs_s[0])
                    load_state(ui + 2)
            pool.wait_ge(sample_state_out, outs_s[0])
            pool.wait_ge(prompt_state_out, 16 * len(HEADS))
            pool.dma_start(rw, a["router_w"]).then_inc(router_landed, 16)
            pool.dma_start(rb, a["router_b"]).then_inc(router_landed, 16)
            pool.dma_start(bdn, a["exp_b_dn"][0, :, :]).then_inc(bdn_landed, 16)
            pool.wait_ge(merged_done, DC)
            for g in range(3):
                pool.dma_start(bguf[32 * g:32 * g + 32, :], a["exp_b_gu"][0, :, :]).then_inc(bgu_landed, 16)

        @block.tensor
        def _(pe):
            mm = nc.tensor.matmul
            ident = C("ident")
            slot = [0]

            def open_turn(name):
                n = TURN[name]
                bank = TURNS[n][2]
                last = [m for m in range(n) if TURNS[m][2] == bank]
                if last:
                    wait_taken(pe, last[-1])
                return banks[bank]

            def sum_squares(name, src, each=None):
                b = open_turn(name)
                for k in range(DC):
                    if each is not None:
                        pe.wait_ge(each, k + 1)
                    last = mm(b[:, 0:T], ones[:, :], src[:, k, :], start=(k == 0), stop=(k == DC - 1))
                last.then_inc(turn_filled, 1)

            def ada(i, between=None):
                b = open_turn(f"ada{i}")
                for k in range(DC):
                    if k == 4 and between:
                        between()
                    landed(pe, slot[0])
                    for g in range(4):
                        last = mm(b[32 * g:32 * g + 32, :], cpad[:, k, :], ring[:, slot[0] % NSLOT, g * 512:(g + 1) * 512],
                                  start=(k == 0), stop=(k == DC - 1))
                    last.then_inc(slot_used if k < DC - 1 else turn_filled, 1)
                    slot[0] += 1

            def ada_flip(i):
                b = open_turn(f"adaT{i}")
                wait_taken(pe, TURN[f"ada{i}"])
                for j in range(4):
                    last = nc.tensor.transpose(b[:, j * P:(j + 1) * P], modsb[:, j * P:(j + 1) * P], ident)
                last.then_inc(turn_filled, 1)

            def input_squares():
                pe.wait_ge(ones_set, 1)
                pe.wait_ge(xsq_ready, 1)
                sum_squares("ss1", hT)

            pe.wait_ge(cond_ready, 1)
            ada(0, input_squares)
            pe.wait_ge(consts_landed, 32)
            ada_flip(0)

            def z_block(name):
                if name[:3] == "low":
                    if name == "low0":
                        pe.wait_ge(w2_landed, 16)
                        wait_taken(pe, TURN["gr"])
                    u = int(name[3])
                    b = open_turn(name)
                    mm(b[:, 0:T], w2[:, u * P:(u + 1) * P], grT[:, :], start=True, stop=True).then_inc(turn_filled, 1)
                    return
                gi = next(g for g in range(6) if name in [x[0] for x in GROUPS[g][2]])
                names = [x[0] for x in GROUPS[gi][2]]
                _, c, w = GROUPS[gi][2][names.index(name)]
                s0 = GROUP_SLOT[gi]
                b = open_turn(name)
                for k in range(DC):
                    if name == names[0] and k % 2 == 0:
                        landed(pe, s0 + k // 2)
                    if name == "hq0" and k % 2 == 0:
                        pe.wait_ge(h_ready, 1 + k // 2)
                    wts = pair(s0 + k // 2)[:, k % 2, c:c + w]
                    if name in ("hi2", "gv2"):
                        t0, tn = TILES[2]
                        for h in range(2):
                            ins = mm(b[64 * h:64 * h + 64, 0:256], hT[:, k, t0:t0 + tn], wts[:, h * 256:(h + 1) * 256],
                                     start=(k == 0), stop=(k == DC - 1))
                    elif name[:2] in ("hi", "gv"):
                        t0, tn = TILES[int(name[2])]
                        ins = mm(b[0:tn, :], hT[:, k, t0:t0 + tn], wts, start=(k == 0), stop=(k == DC - 1))
                    else:
                        ins = mm(b[0:w, 0:T], wts, hT[:, k, :], start=(k == 0), stop=(k == DC - 1))
                    if k == DC - 1:
                        ins.then_inc(turn_filled, 1)
                    elif name == names[-1] and k % 2:
                        ins.then_inc(slot_used, 1)
                if name == names[-1]:
                    slot[0] += 4

            def group(gi):
                for name, _, _ in GROUPS[gi][2]:
                    z_block(name)

            def fill(ui, place):
                for name in FILL.get((ui, place), []):
                    z_block(name)

            group(0)
            ada(1)
            group(1)
            ada_flip(1)
            ada(2)
            ada_flip(2)

            def wait_rec_banks(upto):
                for o in "vs":
                    last = [n for n in range(upto) if TURNS[n][1] == o and TURNS[n][2] in REC_BANKS]
                    wait_taken(pe, last[-1])

            def wait_all_turns():
                for o in "vs":
                    pe.wait_ge(taken[o], sum(1 for _, x, _ in TURNS if x == o))

            bATT, bKD, bO, bU = banks[0], banks[1], banks[2], banks[3:5]

            def recurrence(bi):
                pe.wait_ge(ops_ready, bi + 1)
                pe.wait_ge(pads_set, 1)
                for ui, (b, u) in enumerate(UNITS):
                    if b != bi:
                        continue
                    o = br[b]
                    heads = [h for h in HEADS if h[0] == b and h[1] == u]
                    if ui:
                        pe.wait_ge(kd_copied, ui)
                    for p, (t0, tn) in enumerate(TILES):
                        last = nc.tensor.transpose(bKD[0:tn, p * P:(p + 1) * P], o["kd"][:, u, t0:t0 + tn], ident)
                    last.then_inc(kd_flipped, 1)
                    for (_, _, hh, n, p0, dk) in heads:
                        if n:
                            pe.wait_ge(att_masked, n)
                        for t0, tn in TILES:
                            last = mm(bATT[0:tn, t0:t0 + tn], o["k"][p0:p0 + dk, u, t0:t0 + tn],
                                      o["qs"][p0:p0 + dk, u, t0:t0 + tn], start=True, stop=True)
                        last.then_inc(att_ready, 1)
                    fill(ui, "a")
                    pe.wait_ge(kd_copied, ui + 1)
                    if ui:
                        pe.wait_ge(su_added, heads[0][3])
                    for (_, _, hh, n, p0, dk) in heads:
                        pe.wait_ge(vmask_ready, n + 1)
                        for p in range(2):
                            last = mm(bU[p][p0:p0 + dk, :], kdtok[:, p, p0:p0 + dk],
                                      vmask[bi][p].rearrange("p c v -> p (c v)"), start=True, stop=True)
                        last.then_inc(u_ready, 1)
                        if hh == 0:
                            fill(ui, "u")
                    fill(ui, "b")
                    pe.wait_ge(chain_done, ui + 1)
                    pe.wait_ge(state_landed[ui % 2], STATE_DMAS[ui] * 16)
                    for (_, _, hh, n, p0, dk) in heads:
                        pe.wait_ge(att_masked, n + 1)
                        if n:
                            pe.wait_ge(o_gated, n)
                        for p, (t0, tn) in enumerate(TILES):
                            mm(bO[:, t0:t0 + tn], vtok[:, p, n * P:(n + 1) * P], attT[:, hh, t0:t0 + tn],
                               start=(p == 0), stop=False, skip_group_check=True)
                        for c in range(1, NCH):
                            mm(bO[:, c * CH:(c + 1) * CH], Sst[p0:p0 + dk, c - 1, :], o["q"][p0:p0 + dk, u, c * CH:(c + 1) * CH],
                               start=False, stop=False, skip_group_check=True)
                        for s in range(NSEQ):
                            t0 = TP + s * TSQ
                            last = mm(bO[:, t0:t0 + TSQ], S0[p0:p0 + dk, ui % 2, s, :], o["q"][p0:p0 + dk, u, t0:t0 + TSQ],
                                      start=False, stop=(s == NSEQ - 1), skip_group_check=True)
                        last.then_inc(o_ready, 1)
                        pe.wait_ge(vblk_ready, n + 1)
                        if n and hh:
                            pe.wait_ge(su_added, n)
                        for x in range(2):
                            r0 = 32 * x
                            last = mm(bU[x][p0:p0 + dk, :], kdtok[r0:r0 + 32, 2, p0:p0 + dk],
                                      vblk[r0:r0 + 32, :, :].rearrange("p a b -> p (a b)"), start=True, stop=True,
                                      tile_position=(r0, p0))
                        last.then_inc(su_ready, 1)
                        fill(ui, f"c{hh}")
                        pe.wait_ge(o_squared, n + 1)
                        at = CONST_COLS["head_col"][0] + 8 - n
                        mm(banks[7][0:8, 0:T], consts[:, at:at + 8], osq[:, :], start=(n == 0), stop=(n == 7))\
                            .then_inc(o_summed, 1)

            wait_rec_banks(TURN["gq0"])
            recurrence(0)
            for name in ("ma0", "ma1"):
                z_block(name)
            pe.wait_ge(o_gated, 4)
            pe.wait_ge(su_added, 4)
            for f in range(2, DC):
                z_block(f"ma{f}")
            wait_rec_banks(TURN["mb0"])
            recurrence(1)
            z_block("mb6")
            z_block("mb7")
            pe.wait_ge(o_gated, 8)
            pe.wait_ge(su_added, 8)
            pe.wait_ge(norms_done, 1)
            for n in range(8):
                b = open_turn(f"nrm{n}")
                mm(b[:, 0:T], ident[0:8, n:n + 1].broadcast_to([8, P]), small[0:8, 0:T], start=True, stop=True)\
                    .then_inc(turn_filled, 1)
            wait_taken(pe, TURN["nrm7"])
            for bi, pre in enumerate(("bh", "bg")):
                s0 = slot[0]
                landed(pe, s0)
                landed(pe, s0 + 1)
                for f in range(DC):
                    b = open_turn(f"{pre}{f}")
                    for k in range(H):
                        ins = mm(b[:, 0:T], pair(s0 + k // 2)[:, k % 2, f * P:(f + 1) * P], gates[:, 4 * bi + k, :],
                                 start=(k == 0), stop=(k == H - 1))
                        if k == H - 1:
                            ins.then_inc(turn_filled, 1)
                        elif f == DC - 1 and k == 1:
                            ins.then_inc(slot_used, 1)
                slot[0] += 2
            s0 = slot[0]
            for f in range(DC):
                b = open_turn(f"out{f}")
                for k in range(DC):
                    if f == 0:
                        if k % 2 == 0:
                            landed(pe, s0 + k // 2)
                        pe.wait_ge(merged_done, k + 1)
                    ins = mm(b[:, 0:T], pair(s0 + k // 2)[:, k % 2, f * P:(f + 1) * P], merged[:, k, :],
                             start=(k == 0), stop=(k == DC - 1))
                    if k == DC - 1:
                        ins.then_inc(turn_filled, 1)
                    elif f == DC - 1 and k % 2:
                        ins.then_inc(slot_used, 1)
            sum_squares("ss2", hT, x2sq_ready)

            pe.wait_ge(router_landed, 32)
            b = open_turn("logits")
            for k in range(DC):
                if k % 2 == 0:
                    pe.wait_ge(h2_ready, 1 + k // 2)
                last = mm(b[0:E, 0:T], rw[:, k, :], hT[:, k, :], start=(k == 0), stop=(k == DC - 1))
            last.then_inc(turn_filled, 1)
            b = open_turn("lflip")
            wait_taken(pe, TURN["logits"])
            for p, (t0, tn) in enumerate(TILES):
                last = nc.tensor.transpose(b[0:tn, p * E:(p + 1) * E], logT[:, t0:t0 + tn], ident[0:E, 0:E])
            last.then_inc(turn_filled, 1)
            for p, (t0, tn) in enumerate(TILES):
                for q in range(2):
                    b = open_turn(f"tok{p}{q}")
                    for j in range(4):
                        last = nc.tensor.transpose(b[0:tn, j * P:(j + 1) * P], hT[:, 4 * q + j, t0:t0 + tn], ident)
                    last.then_inc(turn_filled, 1)
            pe.wait_ge(sel_routed, 1)
            b = open_turn("rank")
            for p in range(3):
                for s in range(p + 1):
                    last = mm(b[:, p * E:(p + 1) * E], C("before") if s == p else ones[:, :], sel[:, s, :],
                              start=(s == 0), stop=(s == p))
            last.then_inc(turn_filled, 1)
            for bank in (0, 1, 2):
                wait_taken(pe, [n for n in range(TURN["count"]) if TURNS[n][2] == bank][-1])
            wait_taken(pe, TURN["tok21"])

            def half(k):
                at = (k % 4) * P + (k // 4) * CAP
                return slice(at, at + CAP)

            def gather(j):
                pe.wait_ge(sel_ready, j + 1)
                for p in range(3):
                    for h in range(2):
                        last = mm(banks[0][64 * h:64 * h + 64, :], Sel[:, p, :], h2tok[:, p, h * 512:(h + 1) * 512],
                                  start=(p == 0), stop=(p == 2))
                last.then_inc(gathered, 1)

            def flip_gathered(j):
                pe.wait_ge(gtok_copied, j + 1)
                for x in range(4):
                    last = nc.tensor.transpose(banks[0][:, x * P:(x + 1) * P], gtok[:, x * P:(x + 1) * P], ident)
                last.then_inc(gtok_flipped, 1)

            def scatter(i, fills):
                for n in fills:
                    q, h = n // 2, n % 2
                    if n == 0:
                        pe.wait_ge(dn_copied, i + 1)
                        pe.wait_ge(selw_copied, i + 1)
                    if n >= 6:
                        pe.wait_ge(summed, i * 8 + (n + 6))
                    mm(banks[SCATTER[n]][:, 0:T], dng[64 * h:64 * h + 64, q * P:(q + 1) * P], SelWT[64 * h:64 * h + 64, :],
                       start=True, stop=True).then_inc(scattered, 1)

            def output_biases(fills):
                for n in fills:
                    f = 4 * (n % 2) + n // 2
                    if n == 0:
                        pe.wait_ge(bdn_landed, 16)
                    if n >= 6:
                        pe.wait_ge(summed, n - 2)
                    mm(banks[SCATTER[n]][:, 0:T], bdn[:, f * P:(f + 1) * P], combT, start=True, stop=True)\
                        .then_inc(scattered, 1)

            def tables(part):
                X = NI
                if part == "count":
                    b = open_turn("count")
                    for s in range(3):
                        last = mm(b[:, 0:1], selx[:, s, :], ones[:, 0:1], start=(s == 0), stop=(s == 2))
                    last.then_inc(turn_filled, 1)
                elif part == "place":
                    wait_taken(pe, TURN["count"])
                    b = open_turn("place")
                    mm(b[:, 0:1], C("before"), flag[:, 0, :], start=True, stop=True)
                    mm(b[0:E, 1:2], C("before_e"), flag[:, 0, :], start=True, stop=True)
                    mm(b[0:1, 2:2 + E], flag[:, 0, :], C("upto_e"), start=True, stop=True)
                    mm(b[0:1, 2 + E:3 + E], flag[:, 0, :], ones[:, 0:1], start=True, stop=True).then_inc(turn_filled, 1)
                elif part == "flips":
                    pe.wait_ge(comb_ready, 1)
                    for name, src in (("posT", posm), ("combT", comb)):
                        b = open_turn(name)
                        for p, (t0, tn) in enumerate(TILES):
                            last = nc.tensor.transpose(b[0:E, t0:t0 + tn], src[0:tn, p, :], ident[0:tn, 0:tn])
                        last.then_inc(turn_filled, 1)
                elif part == "items":
                    pe.wait_ge(oq_ready, 1)
                    pe.wait_ge(thr_ready, 1)
                    b = open_turn("xitems")
                    mm(b[0:96, 0:X], C("pick96"), Oq[:, 0, :], start=True, stop=False)
                    mm(b[0:96, 0:X], C("own96", E), Oe[0:E, 0, :], start=False, stop=True)
                    mm(b[0:1, X:2 * X], C("eid"), Oq[:, 0, :], start=True, stop=False)
                    mm(b[0:1, X:2 * X], C("e_col", E), Oe[0:E, 0, :], start=False, stop=True)
                    mm(b[:, 2 * X:3 * X], thrrep[:, 0, :], Oq[:, 0, :], start=True, stop=True).then_inc(turn_filled, 1)
                elif part == "places":
                    pe.wait_ge(xoh_ready, 1)
                    for name, src in (("xpos", posT), ("xcomb", combT)):
                        b = open_turn(name)
                        for p, (t0, tn) in enumerate(TILES):
                            last = mm(b[0:tn, p * X:(p + 1) * X], src[:, t0:t0 + tn], OHI[0:E, :], start=True, stop=True)
                        last.then_inc(turn_filled, 1)

            def item(i, e, first):
                pe.wait_ge(h2g_copied, i + 1)
                pe.wait_ge(bsel_ready, i + 1)
                if not first:
                    pe.wait_ge(gate_clamped, i)
                    pe.wait_ge(act_ready, i)
                for m in range(2):
                    for h in range(2):
                        mm(banks[1 + m][64 * h:64 * h + 64, :], bsel[0:96, :], bgu[0:96, m * D + h * 512:m * D + (h + 1) * 512],
                           start=True, stop=False)
                for k in range(DC):
                    pe.wait_ge(slot_landed[item_slot(k)], e * 16 + item_landed_count(k))
                    for m in range(2):
                        for h in range(2):
                            c = m * D + h * 512
                            ins = mm(banks[1 + m][64 * h:64 * h + 64, :], h2g[:, half(k)],
                                     ring[:, item_slot(k), c:c + 512], start=False, stop=(k == DC - 1))
                        if k == DC - 1:
                            ins.then_inc(up_ready if m else gate_ready, 1)
                        elif m:
                            ins.then_inc(slot_used, 1)
                    if first and k in (1, 3):
                        tables("items" if k == 1 else "places")
                if first:
                    wait_all_turns()
                else:
                    pe.wait_ge(summed, i * 8)
                gather(i + 1)
                add_last = output_biases if first else lambda fills: scatter(i - 1, fills)
                add_last(range(5))
                pe.wait_ge(act_ready, i + 1)
                pe.wait_ge(summed, i * 8 + 1)
                for j in range(4):
                    last = nc.tensor.transpose(banks[3][:, j * P:(j + 1) * P], actb[:, j * P:(j + 1) * P], ident)
                last.then_inc(act_flipped, 1)
                pe.wait_ge(gtok_copied, i + 2)
                add_last(range(5, 8))
                pe.wait_ge(selw_ready, i + 1)
                pe.wait_ge(summed, i * 8 + 2)
                for p, (t0, tn) in enumerate(TILES):
                    last = nc.tensor.transpose(banks[5][:, t0:t0 + tn], SelW[0:tn, p, :], ident[0:tn, 0:tn])
                last.then_inc(selw_flipped, 1)
                pe.wait_ge(act_copied, i + 1)
                pe.wait_ge(summed, i * 8 + 3)
                for k in range(DC):
                    if k % 2 == 0:
                        s = DC + k // 2
                        pe.wait_ge(slot_landed[item_slot(s)], e * 16 + item_landed_count(s))
                    for h in range(2):
                        ins = mm(banks[4][64 * h:64 * h + 64, :], actT[:, half(k)],
                                 pair(item_slot(DC + k // 2))[:, k % 2, h * 512:(h + 1) * 512],
                                 start=(k == 0), stop=(k == DC - 1))
                    if k == 5:
                        ins.then_inc(slot_used, 1)
                        pe.wait_ge(summed, i * 8 + 6)
                        flip_gathered(i + 1)
                        continue
                    if k == DC - 1:
                        ins.then_inc(dn_ready, 1)
                    elif k % 2:
                        ins.then_inc(slot_used, 1)

            tables("count")
            gather(0)
            tables("place")
            flip_gathered(0)
            tables("flips")
            item(0, 0, True)
            count = pe.value_load(itemtab[0:1, NI:NI + 1], min_val=0, max_val=MAXEXTRA) + E
            with pe.Fori(1, count) as i:
                item(i, pe.value_load(itemtab[0:1, ds(i, 1)], min_val=0, max_val=E - 1), False)
            pe.wait_ge(summed, count * 8)
            pe.wait_ge(h2g_copied, count + 1)
            scatter(count - 1, range(8))
            for n in range(8):
                pe.wait_ge(x3sq_ready, n + 1)
                last = mm(banks[1][:, 0:T], ones[:, :], hT[:, 4 * (n % 2) + n // 2, :], start=(n == 0), stop=(n == 7))
            last.then_inc(ss3_ready, 1)

        @block.scalar
        def _(act):
            S = Steps(act, scalar_step)
            A = nc.scalar.activation
            act.dma_start(cT, a["cT"]).then_inc(c_landed, 16)
            act.dma_start(xT[:, :, :], a["xT"]).then_inc(x_landed, 16)
            act.dma_start(consts[:, :], a["consts"]).then_inc(consts_landed, 16)
            act.dma_start(vec[:, :], a["vec"]).then_inc(consts_landed, 16)
            act.wait_ge(c_landed, 16)
            A(csig, cT, ACT.Sigmoid).then_inc(csig_ready, 1)
            act.wait_ge(x_landed, 16)
            A(hT[:, :, :], xT[:, :, :], ACT.Square).then_inc(xsq_ready, 1)

            def copy_mod(i):
                wait_filled(act, f"ada{i}")
                if i:
                    wait_taken(act, TURN[f"adaT{i - 1}"])
                A(modsb, bank_of(f"ada{i}")[:, :], ACT.Copy).then_inc(taken["s"], 1)

            act.wait_ge(lbexp_wanted, 1)
            A(lbt[:, 0:2, :], lbt[:, 0:2, :], ACT.Exp).then_inc(lbexp_ready, 1)
            wait_taken(act, TURN["ss1"])
            A(small[:, 0:T], small[:, 0:T], ACT.Sqrt).then_inc(root_ready, 1)
            copy_mod(0)

            scratch, sig_names = [0], []

            def sig_scratch(name):
                m = scratch[0]
                wait_filled(act, name)
                if m >= 2:
                    wait_taken(act, TURN[sig_names[m - 2]])
                else:
                    act.wait_ge(h_ready, 4)
                sig_names.append(name)
                A(small[:, (m % 2) * T:(m % 2 + 1) * T], bank_of(name)[:, 0:T], ACT.Sigmoid).then_inc(sig_ready, 1)
                scratch[0] += 1

            for u in range(4):
                sig_scratch(f"hq{u}")
            for u in range(4):
                wait_filled(act, f"hf{u}")
                A(br[0]["k"][:, u, :], bank_of(f"hf{u}")[:, 0:T], ACT.Sigmoid).then_inc(taken["s"], 1)

            def branch_exps(bi):
                o = br[bi]
                w0 = 3 * bi
                if bi == 0:
                    act.wait_ge(exp_wanted, 1)
                    A(o["D"], o["D"], ACT.Ln).then_inc(exp_ready, 1)
                for j, (dst, sign) in enumerate((("D", 1.0), ("qs", 1.0), ("D", -1.0), ("D", 1.0))):
                    src = "D" if j < 3 else "B"
                    act.wait_ge(exp_wanted, w0 + (2, 3, 3, 4)[j])
                    if j == 2:
                        act.wait_ge(exp_ready, 6 + 1 if bi else 3)
                    A(o[dst], o[src], ACT.Exp, scale=sign).then_inc(exp_ready, 1)

            branch_exps(0)
            copy_mod(1)

            def copy_v(name, at):
                p = int(name[2])
                wait_filled(act, name)
                if p < 2:
                    ins = A(vtok[:, p, at:at + 512], bank_of(name)[:, :], ACT.Copy)
                else:
                    for h in range(2):
                        ins = A(vtok[0:64, p, at + h * 256:at + (h + 1) * 256], bank_of(name)[64 * h:64 * h + 64, 0:256], ACT.Copy)
                ins.then_inc(taken["s"], 1)

            for p in range(3):
                copy_v(f"hi{p}", 0)
            for u in range(4):
                sig_scratch(f"hg{u}")
            copy_mod(2)

            def empty(name):
                if name[:2] == "gv":
                    copy_v(name, 512)
                elif name[:2] == "gg":
                    sig_scratch(name)
                elif name[:2] == "mb":
                    wait_filled(act, name)
                    A(mb[:, int(name[2]), :], bank_of(name)[:, 0:T], ACT.Sigmoid).then_inc(taken["s"], 1)
                elif name == "low1":
                    act.wait_ge(low_wanted, 1)
                    S.then_wait(A(br[1]["D"], br[1]["D"], ACT.Exp))
                    A(br[1]["D"], br[1]["D"], ACT.Ln, bias=1.0).then_inc(low_ready, 1)

            def fill(ui, *places):
                for place in places:
                    for name in FILL.get((ui, place), []):
                        empty(name)

            def recurrence(bi):
                for ui, (b, u) in enumerate(UNITS):
                    if b != bi:
                        continue
                    heads = [h for h in HEADS if h[0] == b and h[1] == u]
                    act.wait_ge(kd_flipped, ui + 1)
                    if ui:
                        act.wait_ge(su_ready, heads[0][3])
                    A(kdtok[:, 0:2, :].rearrange("p a b -> p (a b)"), banks[1][:, 0:2 * P], ACT.Copy)
                    A(kdtok[0:64, 2, :], banks[1][0:64, 2 * P:3 * P], ACT.Copy).then_inc(kd_copied, 1)
                    fill(ui, "a", "u", "b")
                    for h in heads:
                        n = h[3]
                        act.wait_ge(o_ready, n + 1)
                        if n:
                            act.wait_ge(o_summed, n)
                        A(osq[:, :], banks[2][:, 0:T], ACT.Square).then_inc(o_squared, 1)
                        fill(ui, f"c{h[2]}")

            def sigmoid_ma(f):
                wait_filled(act, f"ma{f}")
                A(ma[:, f, :], bank_of(f"ma{f}")[:, 0:T], ACT.Sigmoid).then_inc(taken["s"], 1)

            recurrence(0)
            sigmoid_ma(0)
            branch_exps(1)
            for f in range(1, DC):
                sigmoid_ma(f)
            recurrence(1)
            act.wait_ge(root_wanted, 1)
            A(small[0:8, 0:T], small[0:8, 0:T], ACT.Sqrt).then_inc(root_ready, 1)
            empty("mb6")
            empty("mb7")
            for f in range(DC):
                act.wait_ge(x_updated, f + 1)
                A(hT[:, f, :], xT[:, f, :], ACT.Square).then_inc(x2sq_ready, 1)
            wait_taken(act, TURN["ss2"])
            A(small[:, 0:T], small[:, 0:T], ACT.Sqrt).then_inc(root_ready, 1)
            act.wait_ge(rexp_wanted, 1)
            A(comb, comb, ACT.Exp).then_inc(rexp_ready, 1)
            for p, (t0, tn) in enumerate(TILES):
                for q in range(2):
                    wait_filled(act, f"tok{p}{q}")
                    A(h2tok[0:tn, p, q * 512:(q + 1) * 512], bank_of(f"tok{p}{q}")[0:tn, :], ACT.Copy).then_inc(taken["s"], 1)

            def copy_gathered(j):
                act.wait_ge(gathered, j + 1)
                A(gtok, banks[0][:, :], ACT.Copy).then_inc(gtok_copied, 1)

            def copy_flipped(j):
                act.wait_ge(gtok_flipped, j + 1)
                A(h2g, banks[0][:, :], ACT.Copy).then_inc(h2g_copied, 1)

            def item(i):
                act.wait_ge(gate_clamped, i + 1)
                A(sbuf_, gbuf, ACT.Sigmoid, scale=ALPHA).then_inc(swish_ready, 1)
                copy_gathered(i + 1)
                act.wait_ge(act_flipped, i + 1)
                A(actT, banks[3][:, :], ACT.Copy).then_inc(act_copied, 1)
                act.wait_ge(selw_flipped, i + 1)
                A(SelWT, banks[5][:, 0:T], ACT.Copy).then_inc(selw_copied, 1)
                copy_flipped(i + 1)
                act.wait_ge(dn_ready, i + 1)
                A(dng, banks[4][:, :], ACT.Copy).then_inc(dn_copied, 1)

            copy_gathered(0)
            copy_flipped(0)
            item(0)
            wait_taken(act, TURN["xitems"])
            count = act.value_load(itemtab[0:1, NI:NI + 1], min_val=0, max_val=MAXEXTRA) + E
            with act.Fori(1, count) as i:
                item(i)
            for n in range(8):
                f = 4 * (n % 2) + n // 2
                act.wait_ge(x3_updated, n + 1)
                A(hT[:, f, :], xT[:, f, :], ACT.Square).then_inc(x3sq_ready, 1)
            act.wait_ge(root3_wanted, 1)
            A(small[:, 0:T], small[:, 0:T], ACT.Sqrt).then_inc(root3_ready, 1)

        @block.vector
        def _(dve):
            S = Steps(dve, vector_step)
            step = S.then_wait
            TT, TS, STT = nc.vector.tensor_tensor, nc.vector.tensor_scalar, nc.vector.scalar_tensor_tensor
            nc.vector.memset(ones[:, :], 1.0).then_inc(ones_set, 1)
            step(nc.vector.memset(cpad, 0.0))
            nc.vector.memset(vtok[64:128, 2, :], 0.0)
            nc.vector.memset(attT[64:128, :, TP:T], 0.0).then_inc(pads_set, 1)
            dve.wait_ge(csig_ready, 1)
            TT(cpad[:, :, 0:NROW], cT, csig, ALU.mult).then_inc(cond_ready, 1)
            dve.wait_ge(consts_landed, 32)
            lb2 = V("lb").rearrange("p (l h) -> p l h", l=2)
            step(TT(lbt[:, 2, :], lb2[:, 0, :], lb2[:, 1, :], ALU.max))
            TT(lbt[:, 0:2, :], lb2, lbt[:, 2:3, :].broadcast_to([P, 2, H]), ALU.subtract).then_inc(lbexp_wanted, 1)
            dve.wait_ge(lbexp_ready, 1)
            step(TT(lbt[:, 2, :], lbt[:, 0, :], lbt[:, 1, :], ALU.add))
            step(nc.vector.reciprocal(lbt[:, 2, :], lbt[:, 2, :]))
            step(TT(lbt[:, 0, :], lbt[:, 0, :], lbt[:, 2, :], ALU.mult))
            step(TS(lbt[:, 1, :], lbt[:, 0, :], -1.0, 1.0, ALU.mult, ALU.add))

            def add_mod_bias(i):
                wait_filled(dve, f"adaT{i}")
                v = bank_of(f"adaT{i}")[:, :].rearrange("p (j g r) -> p j g r", j=4, g=4)[:, :, :, 0:NROW]
                o = modT[:, 16 * i:16 * i + 16, :].rearrange("p (g j) r -> p j g r", j=4)
                bias = V("ada_b")[:, 16 * i:16 * i + 16].rearrange("p (g j) -> p j g", j=4).unsqueeze(3)\
                    .broadcast_to([P, 4, 4, NROW])
                TT(o, v, bias, ALU.add).then_inc(taken["v"], 1)

            def gain(at, name):
                return STT(modT[:, at:at + 8, :], modT[:, at:at + 8, :], 1.0,
                           V(name).unsqueeze(2).broadcast_to([P, 8, NROW]), ALU.add, ALU.mult)

            def modulate(gain, shift, ready, scaled):
                for k0 in range(0, DC, 2):
                    k1 = k0 + 2
                    if not scaled:
                        step(TT(hT[:, k0:k1, :], xT[:, k0:k1, :], spread(r0)[:, k0:k1, :], ALU.mult))
                    hs = hT[:, k0:k1, TP:T].rearrange("p c (b t) -> p c b t", t=TSQ)
                    bs = lambda at: modT[:, at + k0:at + k1, 1:NROW].unsqueeze(3).broadcast_to([P, 2, NSEQ, TSQ])
                    TT(hs, hs, bs(gain), ALU.mult).then_inc(S.sem, 1)
                    S.n += 1
                    for k in range(k0, k1):
                        TS(hT[:, k, 0:TP], hT[:, k, 0:TP], modT[:, gain + k, 0:1], modT[:, shift + k, 0:1], ALU.mult, ALU.add)
                    dve.wait_ge(S.sem, S.base + S.n)
                    TT(hs, hs, bs(shift), ALU.add).then_inc(ready, 1)

            def spread(row):
                return row.unsqueeze(1).broadcast_to([P, DC, T])

            r0 = small[:, 0:T]
            wait_filled(dve, "ss1")
            TS(r0, bank_of("ss1")[:, 0:T], 1.0 / D, EPS, ALU.mult, ALU.add).then_inc(taken["v"], 1)
            dve.wait_ge(root_ready, 1)
            step(nc.vector.reciprocal(r0, r0))
            step(TT(hT[:, :, :], xT[:, :, :], spread(r0), ALU.mult))
            add_mod_bias(0)
            dve.wait_ge(taken["v"], taken_count(TURN["adaT0"]))
            step(gain(8, "norm1"))
            modulate(8, 0, h_ready, True)

            scratch = [0]

            def gated(name, dst, factor):
                m = scratch[0]
                dve.wait_ge(sig_ready, m + 1)
                STT(dst, bank_of(name)[:, 0:T], factor, small[:, (m % 2) * T:(m % 2 + 1) * T], ALU.mult, ALU.mult)\
                    .then_inc(taken["v"], 1)
                scratch[0] += 1

            o = br[0]
            for u in range(4):
                gated(f"hq{u}", o["q"][:, u, :], float(P) ** -0.5)
            dve.wait_ge(taken["s"], taken_count(TURN["hf3"]))
            for u in range(4):
                ins = TS(o["D"][:, u, :], o["k"][:, u, :], lbt[:, 1, u:u + 1], lbt[:, 0, u:u + 1], ALU.mult, ALU.add)
            step(ins)
            TS(o["k"], o["D"], -1.0, 1.0, ALU.mult, ALU.add).then_inc(exp_wanted, 1)

            def branch_operands(bi):
                o = br[bi]
                n = o["n"]
                got = [5 if bi else 1]

                def wait_exp():
                    got[0] += 1
                    dve.wait_ge(exp_ready, got[0])

                if bi == 0:
                    dve.wait_ge(exp_wanted, 1)
                    dve.wait_ge(exp_ready, 1)
                for u in range(n):
                    ins = nc.vector.tensor_tensor_scan(o["B"][:, u, :], C("carry"), o["D"][:, u, :], 0.0, ALU.mult, ALU.add)
                step(ins)

                def parts(ap):
                    return [ap[:, :, 0:TP].rearrange("p u (c t) -> p u c t", t=CH),
                            ap[:, :, TP:T].rearrange("p u (c t) -> p u c t", t=TSQ)]
                Bp, Dp = parts(o["B"]), parts(o["D"])

                def against(pos, flip):
                    for x, (b, d, t) in enumerate(zip(Bp, Dp, (CH, TSQ))):
                        at = (t - 1) if pos == "last" else t // 2 - 1
                        ref = b[:, :, :, at:at + 1].broadcast_to([P, n, NCH, t])
                        ins = TT(d, ref, b, ALU.subtract) if flip else TT(d, b, ref, ALU.subtract)
                    return ins

                against("last", True).then_inc(exp_wanted, 1)
                wait_exp()
                step(TT(o["kd"], o["k"], o["D"], ALU.mult))
                step(against("mid", False))
                TS(o["D"], o["D"], -CLAMP, CLAMP, ALU.max, ALU.min).then_inc(exp_wanted, 1)
                wait_exp()
                step(TT(o["qs"], o["q"], o["qs"], ALU.mult))
                wait_exp()
                TT(o["k"], o["k"], o["D"], ALU.mult).then_inc(exp_wanted, 1)
                wait_exp()
                TT(o["q"], o["q"], o["D"], ALU.mult).then_inc(ops_ready, 1)

            branch_operands(0)
            for h in range(4):
                gated(f"hg{h}", gates[:, h, :], V("hgain"))
            add_mod_bias(1)
            add_mod_bias(2)
            dve.wait_ge(taken["v"], taken_count(TURN["adaT2"]))
            gain(32, "norm2")
            g = br[1]
            small2 = small[:, :].rearrange("p (u t) -> p u t", u=2)

            def empty(name):
                u = int(name[-1]) if name != "gr" else 0
                if name[:2] in ("gq", "gk"):
                    wait_filled(dve, name)
                    TS(g[name[1]][:, u, :], bank_of(name)[:, 0:T], 64.0 ** -0.5 if name[1] == "q" else 1.0, None, ALU.mult)\
                        .then_inc(taken["v"], 1)
                elif name == "gr":
                    wait_filled(dve, name)
                    TS(grT[:, :], bank_of(name)[0:RANK, 0:T], 1.0, None, ALU.mult).then_inc(taken["v"], 1)
                elif name[:2] == "gg":
                    gated(name, gates[:, 4 + u, :], V("ggain"))
                elif name[:3] == "low":
                    if u == 0:
                        dve.wait_ge(taken["v"], taken_count(TURN["gg3"]))
                    wait_filled(dve, name)
                    TS(g["D"][:, u, :], bank_of(name)[:, 0:T], V("gla_b")[:, u:u + 1], None, ALU.add)
                    TS(small2[:, u, :], bank_of(name)[:, 0:T], V("gla_b")[:, u:u + 1], 0.0, ALU.add, ALU.min)\
                        .then_inc(taken["v"], 1)
                if name == "low1":
                    dve.wait_ge(taken["v"], taken_count(TURN["low1"]))
                    STT(g["D"], small2, 2.0, g["D"], ALU.mult, ALU.subtract).then_inc(low_wanted, 1)
                    dve.wait_ge(low_ready, 1)
                    step(TT(g["D"], small2, g["D"], ALU.subtract))
                    step(TS(g["D"], g["D"], 1.0 / GATE_NORM, None, ALU.mult))

            def fill(ui, *places):
                for place in places:
                    for name in FILL.get((ui, place), []):
                        empty(name)

            def mask_chunks(bi, n):
                if n:
                    dve.wait_ge(u_ready, n)
                wait_taken(dve, TURN["gv2" if bi else "hi2"])
                for p in range(2):
                    ins = TT(vmask[bi][p], vtok[:, p, n * P:(n + 1) * P].unsqueeze(1).broadcast_to([P, 4, P]),
                             C("chunk").unsqueeze(2).broadcast_to([P, 4, P]), ALU.mult)
                ins.then_inc(vmask_ready, 1)

            def mask_sequences(bi, n):
                if n:
                    dve.wait_ge(su_ready, n)
                wait_taken(dve, TURN["gv2" if bi else "hi2"])
                TT(vblk[:, :, :], vtok[0:64, 2, n * P:(n + 1) * P].unsqueeze(1).broadcast_to([64, 4, P]),
                   C("seq", 64).unsqueeze(2).broadcast_to([64, 4, P]), ALU.mult).then_inc(vblk_ready, 1)

            def recurrence(bi):
                mask_chunks(bi, 4 * bi)
                mask_sequences(bi, 4 * bi)
                for ui, (b, u) in enumerate(UNITS):
                    if b != bi:
                        continue
                    o = br[b]
                    heads = [h for h in HEADS if h[0] == b and h[1] == u]
                    for (_, _, hh, n, p0, dk) in heads:
                        dve.wait_ge(att_ready, n + 1)
                        if n:
                            dve.wait_ge(o_ready, n - hh)
                        TT(attT[:, hh, 0:TP].rearrange("p (a t) -> p a t", a=2), banks[0][:, 0:TP].rearrange("p (a t) -> p a t", a=2),
                           C("mask_prompt").unsqueeze(1).broadcast_to([P, 2, P]), ALU.mult)
                        TT(attT[0:64, hh, TP:T], banks[0][0:64, TP:T], C("mask_sample", 64), ALU.mult).then_inc(att_masked, 1)
                    fill(ui, "a", "u")
                    last = heads[-1][3]
                    if len(heads) > 1:
                        mask_chunks(bi, last)
                    dve.wait_ge(u_ready, last + 1)
                    if ui:
                        dve.wait_ge(prompt_state_out, 16 * FIRSTHEAD[ui])
                    step(TS(Sst[:, 0, :], banks[3][:, 0:P], 1.0, None, ALU.mult))
                    for c in range(1, NCH):
                        ins = STT(Sst[:, c, :], Sst[:, c - 1, :], o["D"][:, u, c * CH + CH - 1:c * CH + CH],
                                  banks[3 + c // 4][:, (c % 4) * P:(c % 4 + 1) * P], ALU.mult, ALU.add)
                        if c < NCH - 1:
                            step(ins)
                    ins.then_inc(chain_done, 1)
                    if last % 4 < 3:
                        mask_chunks(bi, last + 1)
                    fill(ui, "b")
                    for (_, _, hh, n, p0, dk) in heads:
                        dve.wait_ge(o_squared, n + 1)
                        TT(gates[:, n, :], gates[:, n, :], banks[2][:, 0:T], ALU.mult).then_inc(o_gated, 1)
                        dve.wait_ge(su_ready, n + 1)
                        for s in range(NSEQ):
                            t1 = TP + s * TSQ + TSQ - 1
                            st = S0[p0:p0 + dk, ui % 2, s, :]
                            ins = STT(st, st, o["D"][p0:p0 + dk, u, t1:t1 + 1],
                                      banks[3 + s // 4][p0:p0 + dk, (s % 4) * P:(s % 4 + 1) * P], ALU.mult, ALU.add)
                        ins.then_inc(su_added, 1)
                        if n % 4 < 3:
                            mask_sequences(bi, n + 1)
                        fill(ui, f"c{hh}")

            recurrence(0)
            branch_operands(1)
            recurrence(1)
            r8 = small[0:8, 0:T]
            dve.wait_ge(o_summed, 8)
            TS(r8, banks[7][0:8, 0:T], 1.0 / P, EPS, ALU.mult, ALU.add).then_inc(root_wanted, 1)
            dve.wait_ge(root_ready, 2)
            nc.vector.reciprocal(r8, r8).then_inc(norms_done, 1)
            for n in range(8):
                wait_filled(dve, f"nrm{n}")
                TT(gates[:, n, :], gates[:, n, :], bank_of(f"nrm{n}")[:, 0:T], ALU.mult).then_inc(taken["v"], 1)
            dve.wait_ge(taken["s"], taken_count(TURN["mb7"]))
            for f in range(DC):
                wait_filled(dve, f"bh{f}")
                TT(merged[:, f, :], ma[:, f, :], bank_of(f"bh{f}")[:, 0:T], ALU.mult).then_inc(taken["v"], 1)
            for f in range(DC):
                wait_filled(dve, f"bg{f}")
                TT(mb[:, f, :], mb[:, f, :], bank_of(f"bg{f}")[:, 0:T], ALU.mult).then_inc(taken["v"], 1)
                dve.wait_ge(taken["v"], taken_count(TURN[f"bg{f}"]))
                TT(merged[:, f, :], merged[:, f, :], mb[:, f, :], ALU.add).then_inc(merged_done, 1)

            def split_bias(part):
                if part == 0:
                    dve.wait_ge(bgu_landed, 48)
                    step(TS(bgu[0:96, :], bguf, 1.0, None, ALU.mult))
                elif part == 1:
                    step(TT(bguf, bguf, bgu[0:96, :], ALU.subtract))
                elif part == 2:
                    TS(bgu[32:64, :], bguf[32:64, :], 1.0, None, ALU.mult)
                    step(TS(bgu[64:96, :], bguf[64:96, :], 1.0, None, ALU.mult))
                elif part == 3:
                    step(TT(bguf[64:96, :], bguf[64:96, :], bgu[64:96, :], ALU.subtract))
                    step(TS(bgu[64:96, :], bguf[64:96, :], 1.0, None, ALU.mult))

            for f in range(DC):
                wait_filled(dve, f"out{f}")
                b = bank_of(f"out{f}")
                if f:
                    dve.wait_ge(x_updated, f)
                step(TT(small[:, 0:TP // 4].rearrange("p (b t) -> p b t", t=TSQ), b[:, TP:T].rearrange("p (b t) -> p b t", t=TSQ),
                        modT[:, 16 + f, 1:NROW].unsqueeze(2).broadcast_to([P, NSEQ, TSQ]), ALU.mult))
                STT(xT[:, f, 0:TP], b[:, 0:TP], modT[:, 16 + f, 0:1], xT[:, f, 0:TP], ALU.mult, ALU.add).then_inc(taken["v"], 1)
                TT(xT[:, f, TP:T], xT[:, f, TP:T], small[:, 0:TP // 4], ALU.add).then_inc(x_updated, 1)
                if 3 <= f < 7:
                    split_bias(f - 3)
            wait_filled(dve, "ss2")
            TS(r0, bank_of("ss2")[:, 0:T], 1.0 / D, EPS, ALU.mult, ALU.add).then_inc(taken["v"], 1)
            dve.wait_ge(root_ready, 3)
            step(nc.vector.reciprocal(r0, r0))
            dve.wait_ge(router_landed, 32)
            modulate(32, 24, h2_ready, False)

            step(nc.vector.memset(Lg[64:128, 2, :], 0.0))
            wait_filled(dve, "logits")
            TS(logT, bank_of("logits")[0:E, 0:T], rb, None, ALU.add).then_inc(taken["v"], 1)
            wait_filled(dve, "lflip")
            b = bank_of("lflip")
            TS(Lg[:, 0:2, :], b[:, 0:2 * E].rearrange("p (a e) -> p a e", a=2), 1.0, None, ALU.mult)
            TS(Lg[0:64, 2, :], b[0:64, 2 * E:3 * E], 1.0, None, ALU.mult).then_inc(taken["v"], 1)
            dve.wait_ge(taken["v"], taken_count(TURN["lflip"]))
            for p in range(3):
                ins = nc.vector.max(top8[:, p, :], Lg[:, p, :])
            step(ins)
            be = lambda m: m.broadcast_to([P, 3, E])
            v1, v4 = top8[:, :, 0:1], top8[:, :, TOPK - 1:TOPK]
            TT(comb, Lg, be(v1), ALU.subtract).then_inc(rexp_wanted, 1)
            TT(sel, Lg, be(v4), ALU.is_gt)
            step(TT(eqm, Lg, be(v4), ALU.is_equal))
            step(nc.vector.tensor_reduce(ngt, sel, AX, ALU.add))
            step(TS(ngt, ngt, -1.0, TOPK + 0.5, ALU.mult, ALU.add))
            for p in range(3):
                ins = nc.vector.tensor_tensor_scan(cum[:, p, :], ones[:, 0:E], eqm[:, p, :], 0.0, ALU.mult, ALU.add)
            step(ins)
            step(TT(cum, cum, be(ngt), ALU.is_lt))
            step(TT(eqm, eqm, cum, ALU.mult))
            step(TT(sel, sel, eqm, ALU.add))
            step(nc.vector.memset(sel[64:128, 2, :], 0.0))
            for p in range(3):
                ins = TT(selx[:, p, :].rearrange("p (e k) -> p e k", k=P // E), sel[:, p, :].unsqueeze(2).broadcast_to([P, E, P // E]),
                         ones[:, :].rearrange("p (e k) -> p e k", k=P // E), ALU.mult)
            ins.then_inc(sel_routed, 1)
            dve.wait_ge(rexp_ready, 1)
            step(TT(comb, comb, sel, ALU.mult))
            step(nc.vector.tensor_reduce(tot, comb, AX, ALU.add))
            step(nc.vector.tensor_scalar(tot, tot, 1e-30, None, ALU.max))
            step(nc.vector.reciprocal(tot, tot))
            step(TT(comb, comb, be(tot), ALU.mult))
            wait_filled(dve, "rank")
            TS(posm, bank_of("rank")[:, 0:3 * E].rearrange("p (a e) -> p a e", a=3), 1.0, None, ALU.add).then_inc(taken["v"], 1)
            dve.wait_ge(taken["v"], taken_count(TURN["rank"]))
            step(TT(posm, posm, sel, ALU.mult))
            TS(posm, posm, -1.0, None, ALU.add).then_inc(comb_ready, 1)
            dve.wait_ge(comb_ready, 1)
            for p in range(3):
                ins = TS(Sel[:, p, :], C("slot_no")[:, 0:CAP], posm[:, p, 0:1], None, ALU.is_equal)
            ins.then_inc(sel_ready, 1)
            TS(bsel[0:96, :], ones[0:96, 0:CAP], C("first96", 96), None, ALU.mult).then_inc(bsel_ready, 1)
            wait_filled(dve, "count")
            TS(flag[:, 0, :], bank_of("count")[:, 0:1], C("thr"), None, ALU.is_gt).then_inc(taken["v"], 1)
            TT(thrrep[:, 0, :], C("thr").broadcast_to([P, P]), ones[:, :], ALU.mult).then_inc(thr_ready, 1)
            wait_filled(dve, "place")
            dve.wait_ge(taken["v"], taken_count(TURN["count"]))
            b = bank_of("place")
            TT(slotq[:, 0, :], b[:, 0:1], C("next_eid"), ALU.add)
            step(TT(starts[0:E, 0, :], b[0:E, 1:2], C("e_col", E), ALU.add))
            TT(itemtab[0:1, NI + 1:NI + 1 + E], b[0:1, 2:2 + E], C("e_row", 1), ALU.add)
            TS(itemtab[0:1, NI:NI + 1], b[0:1, 2 + E:3 + E], 1.0, None, ALU.mult).then_inc(taken["v"], 1)
            TS(Oe[0:E, 0, :], C("item_no", E), starts[0:E, 0, :], None, ALU.is_equal)
            TS(Oq[:, 0, :], C("item_no"), slotq[:, 0, :], flag[:, 0, :], ALU.is_equal, ALU.mult).then_inc(oq_ready, 1)
            for name, dst in (("posT", posT), ("combT", combT)):
                wait_filled(dve, name)
                TS(dst, bank_of(name)[0:E, 0:T], 1.0, None, ALU.mult).then_inc(taken["v"], 1)
            dve.wait_ge(comb_ready, 1)
            nc.vector.memset(posI[64:128, 2, :], -1.0)
            nc.vector.memset(wI[64:128, 2, :], 0.0)
            X = NI
            wait_filled(dve, "xitems")
            b = bank_of("xitems")
            TS(OHI[0:96, :], b[0:96, 0:X], 1.0, None, ALU.mult).then_inc(xoh_ready, 1)
            TS(itemtab[0:1, 0:NI], b[0:1, X:2 * X], 1.0, None, ALU.mult)
            TS(frow[:, 0, :], b[:, 2 * X:3 * X], 1.0, None, ALU.mult).then_inc(taken["v"], 1)
            wait_filled(dve, "xpos")
            dve.wait_ge(taken["v"], taken_count(TURN["xitems"]))
            b = bank_of("xpos")
            TT(posI[:, 0:2, :], b[:, 0:2 * X].rearrange("p (a i) -> p a i", a=2), frow.broadcast_to([P, 2, X]), ALU.subtract)
            TT(posI[0:64, 2, :], b[0:64, 2 * X:3 * X], frow[0:64, 0, :], ALU.subtract).then_inc(taken["v"], 1)
            wait_filled(dve, "xcomb")
            b = bank_of("xcomb")
            TS(wI[:, 0:2, :], b[:, 0:2 * X].rearrange("p (a i) -> p a i", a=2), 1.0, None, ALU.mult)
            TS(wI[0:64, 2, :], b[0:64, 2 * X:3 * X], 1.0, None, ALU.mult).then_inc(taken["v"], 1)
            dve.wait_ge(taken["v"], taken_count(len(TURNS) - 1))

            def col(tab, p, j):
                return tab[:, p, j:j + 1] if isinstance(j, int) else tab[:, p, ds(j, 1)]

            def select(j):
                for p in range(3):
                    ins = TS(Sel[:, p, :], C("slot_no")[:, 0:CAP], col(posI, p, j), None, ALU.is_equal)
                ins.then_inc(sel_ready, 1)

            def select_bias(j):
                c = OHI[0:96, j:j + 1] if isinstance(j, int) else OHI[0:96, ds(j, 1)]
                TS(bsel[0:96, :], ones[0:96, 0:CAP], c, None, ALU.mult).then_inc(bsel_ready, 1)

            def add_scattered(i):
                dve.wait_ge(summed, i * 8 + 8)
                for q in range(4):
                    for h in range(2):
                        n = 2 * q + h
                        dve.wait_ge(scattered, i * 8 + (n + 9))
                        f = 4 * h + q
                        TT(yacc[:, f, :], yacc[:, f, :], banks[SCATTER[n]][:, 0:T], ALU.add).then_inc(summed, 1)

            def item(i, first):
                dve.wait_ge(gathered, i + 1)
                select(i + 1)
                if not first:
                    dve.wait_ge(selw_flipped, i)
                for p in range(3):
                    ins = TS(SelW[:, p, :], C("slot_no"), col(posI, p, i), col(wI, p, i), ALU.is_equal, ALU.mult)
                ins.then_inc(selw_ready, 1)
                dve.wait_ge(gate_ready, i + 1)
                TS(gbuf, banks[1][:, :], LIMIT, None, ALU.min).then_inc(gate_clamped, 1)
                dve.wait_ge(up_ready, i + 1)
                if not first:
                    dve.wait_ge(act_ready, i)
                step(TS(ubuf, banks[2][:, :], -LIMIT, LIMIT, ALU.max, ALU.min))
                step(STT(ubuf, ubuf, 1.0, gbuf, ALU.add, ALU.mult))
                dve.wait_ge(swish_ready, i + 1)
                TT(actb, ubuf, sbuf_, ALU.mult).then_inc(act_ready, 1)
                select_bias(i + 1)
                if first:
                    for n in range(8):
                        dve.wait_ge(scattered, n + 1)
                        TS(yacc[:, 4 * (n % 2) + n // 2, :], banks[SCATTER[n]][:, 0:T], 1.0, None, ALU.mult).then_inc(summed, 1)
                else:
                    add_scattered(i - 1)

            PER_ITEM = 2
            item(0, True)
            n0 = S.n
            count = dve.value_load(itemtab[0:1, NI:NI + 1], min_val=0, max_val=MAXEXTRA) + E
            with dve.Fori(1, count) as i:
                S.base = (i - 1) * PER_ITEM
                item(i, False)
                assert S.n == n0 + PER_ITEM
            S.base = (count - 2) * PER_ITEM
            dve.wait_ge(summed, count * 8)

            def samples(ap):
                return ap.rearrange("p c (b t) -> p c b t", t=TSQ)

            step(TT(samples(yacc[:, :, TP:T]), samples(yacc[:, :, TP:T]),
                    modT[:, 40:48, 1:NROW].unsqueeze(3).broadcast_to([P, DC, NSEQ, TSQ]), ALU.mult))
            for f in range(DC):
                STT(xT[:, f, 0:TP], yacc[:, f, 0:TP], modT[:, 40 + f, 0:1], xT[:, f, 0:TP], ALU.mult, ALU.add)
            step(TT(xT[:, :, TP:T], xT[:, :, TP:T], yacc[:, :, TP:T], ALU.add))
            for n in range(8):
                f = 4 * (n % 2) + n // 2
                dve.wait_ge(scattered, count * 8 + (n + 1))
                b = banks[SCATTER[n]]
                TT(yacc[:, f, TP:T].rearrange("p (b t) -> p b t", t=TSQ), b[:, TP:T].rearrange("p (b t) -> p b t", t=TSQ),
                   modT[:, 40 + f, 1:NROW].unsqueeze(2).broadcast_to([P, NSEQ, TSQ]), ALU.mult).then_inc(S.sem, 1)
                S.n += 1
                STT(xT[:, f, 0:TP], b[:, 0:TP], modT[:, 40 + f, 0:1], xT[:, f, 0:TP], ALU.mult, ALU.add).then_inc(summed, 1)
                dve.wait_ge(S.sem, S.base + S.n)
                TT(xT[:, f, TP:T], xT[:, f, TP:T], yacc[:, f, TP:T], ALU.add).then_inc(x3_updated, 1)
            dve.wait_ge(ss3_ready, 1)
            TS(r0, banks[1][:, 0:T], 1.0 / D, EPS, ALU.mult, ALU.add).then_inc(root3_wanted, 1)
            dve.wait_ge(root3_ready, 1)
            step(nc.vector.reciprocal(r0, r0))
            for f in range(DC):
                ins = STT(xT[:, f, :], xT[:, f, :], V("final")[:, f:f + 1], r0, ALU.mult, ALU.mult)
                if f % 2:
                    ins.then_inc(y_ready, 1)



def kernel(**inputs):
    import numpy as _np
    import concourse.bacc as _bacc
    from concourse import mybir as _mybir
    from concourse.bass_utils import run_bass_kernel_spmd as _run

    def fm(v):
        return _np.asarray(v).reshape(-1, P).T

    g = {k: _np.asarray(v) for k, v in inputs.items()}
    x = _np.concatenate([g["x_prompt"].reshape(TP, D), g["x_sample"].reshape(NSEQ * TSQ, D)])
    c = _np.concatenate([g["c_prompt"], g["c_sample"]])
    vec = _np.concatenate([fm(g["ada_b"][0]), fm(g["norm1_g"][0]), fm(g["norm2_g"][0]), fm(g["final_g"]),
                           fm(g["hgrn_lb"].reshape(-1)), fm(g["hgrn_norm_g"][0]), fm(g["gla_norm_g"][0]),
                           fm(g["gla_gate_b"][0])], 1)
    arrays = {
        "xT": x.reshape(T, DC, P).transpose(2, 1, 0),
        "cT": c.reshape(NROW, DC, P).transpose(2, 1, 0),
        "vec": vec,
        "consts": CONSTS,
        "gla_w2": g["gla_gate_w2"][0],
        "router_w": g["router_w"][0].reshape(DC, P, E).transpose(1, 0, 2),
        "router_b": g["router_b"].reshape(E, 1),
    }
    for name in ("state_hgrn", "state_gla", "ada_w", "w_in", "w_branch_h", "w_branch_g", "w_out",
                 "exp_w_gu", "exp_b_gu", "exp_w_dn", "exp_b_dn"):
        arrays[name] = g[name]
    arrays = {k: _np.ascontiguousarray(v) for k, v in arrays.items()}
    outs = {"yT": (P, DC, T), "hgrn_prompt": (1, 1, H, 128, 128), "gla_prompt": (1, 1, H, 64, 128),
            "hgrn_sample": (1, NSEQ, H, 128, 128), "gla_sample": (1, NSEQ, H, 64, 128)}
    nc = _bacc.Bacc("TRN2", target_bir_lowering=False, num_devices=1)
    aps = {k: nc.dram_tensor(f"in_{k}", v.shape, _mybir.dt.from_np(v.dtype), kind="ExternalInput").ap()
           for k, v in arrays.items()}
    for k, s in outs.items():
        aps[k] = nc.dram_tensor(f"out_{k}", s, _mybir.dt.float32, kind="ExternalOutput").ap()
    build(nc, aps)
    r = _run(nc, [{f"in_{k}": v for k, v in arrays.items()}], core_ids=[0]).results[0]
    y = r["out_yT"].transpose(2, 1, 0).reshape(T, D)
    return (y[:TP].reshape(1, TP, D), y[TP:].reshape(NSEQ, TSQ, D), r["out_hgrn_prompt"], r["out_gla_prompt"],
            r["out_hgrn_sample"], r["out_gla_sample"])
```
